# Optimizing a Trainium2 kernel written in Bass

```python
import jax, jax.numpy as jnp
from jax import lax
import numpy as np

D_MODEL = 1024
BATCH = 1
SEQ = 512
DEPTH = 1

D_MIX = D_MODEL
GDN_HEADS = 4
GDN_DK = 128
GDN_DV = 128
GDN_QK = GDN_HEADS * GDN_DK
GDN_V = GDN_HEADS * GDN_DV
GDN_CONV = 4
GDN_CHUNK = 64
CF_CH = D_MIX - GDN_V
CF_KERNEL = 31
N_EXPERTS = 32
TOP_K = 4
D_FF = D_MODEL
SWIGLU_LIMIT = 7.0
SWIGLU_ALPHA = 1.702
MOE_BLOCK = 128
NORM_EPS = 1e-6

OFF_Q = 0
OFF_K = OFF_Q + GDN_QK
OFF_V = OFF_K + GDN_QK
OFF_Z = OFF_V + GDN_V
OFF_B = OFF_Z + GDN_V
OFF_A = OFF_B + GDN_HEADS
OFF_CF = OFF_A + GDN_HEADS
IN_COLS = OFF_CF + 2 * CF_CH

kernel_name = "hybrid_gdn_conformer_moe_block"

def _rmsnorm(x, w):
    xf = x.astype(jnp.float32)
    y = xf * lax.rsqrt(jnp.mean(xf * xf, axis=-1, keepdims=True) + NORM_EPS)
    return (y * w.astype(jnp.float32)).astype(x.dtype)

def _layernorm(x, w, b):
    xf = x.astype(jnp.float32)
    mu = jnp.mean(xf, axis=-1, keepdims=True)
    xc = xf - mu
    y = xc * lax.rsqrt(jnp.mean(xc * xc, axis=-1, keepdims=True) + NORM_EPS)
    return (y * w.astype(jnp.float32) + b.astype(jnp.float32)).astype(x.dtype)

def _gated_rmsnorm(o, w, z):
    of = o.astype(jnp.float32)
    y = of * lax.rsqrt(jnp.mean(of * of, axis=-1, keepdims=True) + NORM_EPS) * w.astype(jnp.float32)
    return (y * jax.nn.silu(z.astype(jnp.float32))).astype(z.dtype)

def _l2norm(t):
    return t * lax.rsqrt(jnp.sum(t * t, axis=-1, keepdims=True) + NORM_EPS)

def _causal_dwconv(x, w):
    width, ch = w.shape
    return lax.conv_general_dilated(
        x, w[:, None, :].astype(x.dtype), window_strides=(1,), padding=[(width - 1, 0)],
        dimension_numbers=("NWC", "WIO", "NWC"), feature_group_count=ch)

def _chunked_gated_delta_rule(q, k, v, g, beta):
    f32 = jnp.float32
    b, s, h, dk = q.shape
    dv = v.shape[-1]
    c = GDN_CHUNK
    n = s // c
    q = q.astype(f32) * (dk ** -0.5)
    k, v, g, beta = k.astype(f32), v.astype(f32), g.astype(f32), beta.astype(f32)

    def chunks(t):
        return t.reshape(b, n, c, h, -1).transpose(0, 3, 1, 2, 4)

    q, k, v = chunks(q), chunks(k), chunks(v)
    g = g.reshape(b, n, c, h).transpose(0, 3, 1, 2)
    beta = beta.reshape(b, n, c, h).transpose(0, 3, 1, 2)
    g = jnp.cumsum(g, axis=-1)

    causal = jnp.tril(jnp.ones((c, c), dtype=bool))
    strict = jnp.tril(jnp.ones((c, c), dtype=bool), k=-1)
    diff = g[..., :, None] - g[..., None, :]
    decay = jnp.exp(jnp.where(causal, diff, -jnp.inf))

    kb = k * beta[..., None]
    vb = v * beta[..., None]
    a_strict = jnp.where(strict, jnp.einsum("bhncd,bhnmd->bhncm", kb, k) * decay, 0.0)
    lower = jnp.eye(c, dtype=f32) + a_strict
    rhs = jnp.concatenate([vb, kb * jnp.exp(g)[..., None]], axis=-1)
    sol = lax.linalg.triangular_solve(lower, rhs, left_side=True, lower=True, unit_diagonal=True)
    u_val = sol[..., :dv]
    w_key = sol[..., dv:]

    intra = jnp.einsum("bhncd,bhnmd->bhncm", q, k) * decay
    q_dec = q * jnp.exp(g)[..., None]
    k_tail = k * jnp.exp(g[..., -1:] - g)[..., None]
    g_tot = jnp.exp(g[..., -1])

    xs = tuple(jnp.moveaxis(t, 2, 0) for t in (u_val, w_key, q_dec, k_tail, intra, g_tot))

    def step(state, inp):
        u_c, w_c, qd_c, kt_c, in_c, gt_c = inp
        v_new = u_c - jnp.einsum("bhcd,bhde->bhce", w_c, state)
        o_c = jnp.einsum("bhcd,bhde->bhce", qd_c, state) + jnp.einsum("bhcm,bhme->bhce", in_c, v_new)
        state = state * gt_c[..., None, None] + jnp.einsum("bhcd,bhce->bhde", kt_c, v_new)
        return state, o_c

    state0 = jnp.zeros((b, h, dk, dv), f32)
    _, o = lax.scan(step, state0, xs)
    return o.transpose(1, 0, 3, 2, 4).reshape(b, s, h, dv)

def _moe(xn, w_router, b_router, w_gate_up, b_gate_up, w_down, b_down):
    b, s, d = xn.shape
    t = b * s
    xt = xn.reshape(t, d)
    logits = (xt @ w_router + b_router).astype(jnp.float32)
    top_val, top_idx = lax.top_k(logits, TOP_K)
    gates = jax.nn.softmax(top_val, axis=-1)

    p = t * TOP_K
    e_flat = top_idx.reshape(p).astype(jnp.int32)
    tok_flat = jnp.arange(p, dtype=jnp.int32) // TOP_K
    g_flat = gates.reshape(p)
    order = jnp.argsort(e_flat)
    e_s, tok_s, g_s = e_flat[order], tok_flat[order], g_flat[order]

    counts = jnp.bincount(e_s, length=N_EXPERTS).astype(jnp.int32)
    padded = ((counts + MOE_BLOCK - 1) // MOE_BLOCK) * MOE_BLOCK
    start = jnp.cumsum(counts) - counts
    pend = jnp.cumsum(padded)
    pstart = pend - padded
    dest = pstart[e_s] + (jnp.arange(p, dtype=jnp.int32) - start[e_s])

    n_blocks = -(-p // MOE_BLOCK) + N_EXPERTS
    rows = n_blocks * MOE_BLOCK
    row_tok = jnp.full((rows,), t, jnp.int32).at[dest].set(tok_s)
    row_gate = jnp.zeros((rows,), jnp.float32).at[dest].set(g_s)
    blk_start = jnp.arange(n_blocks, dtype=jnp.int32) * MOE_BLOCK
    blk_exp = jnp.minimum(jnp.searchsorted(pend, blk_start, side="right"), N_EXPERTS - 1)

    x_pad = jnp.concatenate([xt, jnp.zeros((1, d), xt.dtype)], axis=0)
    xb = x_pad[row_tok].reshape(n_blocks, MOE_BLOCK, d)

    def expert_block(args):
        x_blk, e = args
        hid = x_blk @ w_gate_up[e] + b_gate_up[e]
        gate, up = hid[:, :D_FF], hid[:, D_FF:]
        gate = jnp.minimum(gate, SWIGLU_LIMIT)
        up = jnp.clip(up, -SWIGLU_LIMIT, SWIGLU_LIMIT)
        glu = gate * jax.nn.sigmoid(SWIGLU_ALPHA * gate)
        return ((up + 1.0) * glu) @ w_down[e] + b_down[e]

    yb = lax.map(expert_block, (xb, blk_exp))
    weighted = yb.reshape(rows, d).astype(jnp.float32) * row_gate[:, None]
    y = jax.ops.segment_sum(weighted, row_tok, num_segments=t + 1)[:t]
    return y.astype(xn.dtype).reshape(b, s, d)

def setup_inputs(seed: int = 0) -> dict:
    key = jax.random.key(seed)
    ks = jax.random.split(key, 20)
    f32 = jnp.float32
    nrm = lambda k, shape, sc: jax.random.normal(k, shape, f32) * sc
    return {
        "x": jax.random.normal(ks[0], (BATCH, SEQ, D_MODEL), f32),
        "attn_norm_w": 1.0 + nrm(ks[1], (DEPTH, D_MODEL), 0.02),
        "w_in": nrm(ks[2], (DEPTH, D_MODEL, IN_COLS), D_MODEL ** -0.5),
        "gdn_conv_w": nrm(ks[3], (DEPTH, GDN_CONV, 2 * GDN_QK + GDN_V), GDN_CONV ** -0.5),
        "gdn_a_log": jnp.log(jax.random.uniform(ks[4], (DEPTH, GDN_HEADS), f32, 1.0, 16.0)),
        "gdn_dt_bias": nrm(ks[5], (DEPTH, GDN_HEADS), 0.1),
        "gdn_norm_w": 1.0 + nrm(ks[6], (DEPTH, GDN_DV), 0.02),
        "cf_dw_w": nrm(ks[7], (DEPTH, CF_KERNEL, CF_CH), CF_KERNEL ** -0.5),
        "cf_dw_b": nrm(ks[8], (DEPTH, CF_CH), 0.02),
        "cf_ln_w": 1.0 + nrm(ks[9], (DEPTH, CF_CH), 0.02),
        "cf_ln_b": nrm(ks[10], (DEPTH, CF_CH), 0.02),
        "w_out": nrm(ks[11], (DEPTH, D_MIX, D_MODEL), D_MIX ** -0.5),
        "ffn_norm_w": 1.0 + nrm(ks[12], (DEPTH, D_MODEL), 0.02),
        "w_router": nrm(ks[13], (DEPTH, D_MODEL, N_EXPERTS), D_MODEL ** -0.5),
        "b_router": nrm(ks[14], (DEPTH, N_EXPERTS), 0.01),
        "w_gate_up": nrm(ks[15], (DEPTH, N_EXPERTS, D_MODEL, 2 * D_FF), D_MODEL ** -0.5),
        "b_gate_up": nrm(ks[16], (DEPTH, N_EXPERTS, 2 * D_FF), 0.02),
        "w_down": nrm(ks[17], (DEPTH, N_EXPERTS, D_FF, D_MODEL), D_FF ** -0.5),
        "b_down": nrm(ks[18], (DEPTH, N_EXPERTS, D_MODEL), 0.02),
        "final_norm_w": 1.0 + nrm(ks[19], (D_MODEL,), 0.02),
    }

def reference(x, attn_norm_w, w_in, gdn_conv_w, gdn_a_log, gdn_dt_bias, gdn_norm_w,
              cf_dw_w, cf_dw_b, cf_ln_w, cf_ln_b, w_out, ffn_norm_w, w_router, b_router,
              w_gate_up, b_gate_up, w_down, b_down, final_norm_w):
    b, s, _ = x.shape
    for l in range(DEPTH):
        h = _rmsnorm(x, attn_norm_w[l])
        proj = h @ w_in[l]

        qkv = jax.nn.silu(_causal_dwconv(proj[..., OFF_Q:OFF_Z], gdn_conv_w[l]))
        q = _l2norm(qkv[..., :GDN_QK].astype(jnp.float32).reshape(b, s, GDN_HEADS, GDN_DK))
        k = _l2norm(qkv[..., GDN_QK:2 * GDN_QK].astype(jnp.float32).reshape(b, s, GDN_HEADS, GDN_DK))
        v = qkv[..., 2 * GDN_QK:].reshape(b, s, GDN_HEADS, GDN_DV)
        z = proj[..., OFF_Z:OFF_B].reshape(b, s, GDN_HEADS, GDN_DV)
        beta = jax.nn.sigmoid(proj[..., OFF_B:OFF_A].astype(jnp.float32))
        g = -jnp.exp(gdn_a_log[l].astype(jnp.float32)) * jax.nn.softplus(
            proj[..., OFF_A:OFF_CF].astype(jnp.float32) + gdn_dt_bias[l].astype(jnp.float32))
        o = _chunked_gated_delta_rule(q, k, v, g, beta)
        out_a = _gated_rmsnorm(o, gdn_norm_w[l], z).reshape(b, s, GDN_V)

        cf = proj[..., OFF_CF:]
        u = cf[..., :CF_CH] * jax.nn.sigmoid(cf[..., CF_CH:])
        u = _causal_dwconv(u, cf_dw_w[l]) + cf_dw_b[l]
        u = jax.nn.silu(_layernorm(u, cf_ln_w[l], cf_ln_b[l]))

        mix = jnp.concatenate([out_a.astype(x.dtype), u.astype(x.dtype)], axis=-1)
        x = x + mix @ w_out[l]

        x = x + _moe(_rmsnorm(x, ffn_norm_w[l]), w_router[l], b_router[l],
                     w_gate_up[l], b_gate_up[l], w_down[l], b_down[l])
    return _rmsnorm(x, final_norm_w)


_drawn_inputs = setup_inputs


def setup_inputs(seed=0):
    import zlib

    import numpy as np

    out = dict(_drawn_inputs(seed))
    spreads = {}
    factors = {'gdn_dt_bias': 4.383, 'b_gate_up': 5.714, 'b_down': 6.606, 'final_norm_w': 2.831}
    for name, (base, spread) in spreads.items():
        noise = np.random.default_rng([zlib.crc32(name.encode()), seed]).standard_normal(out[name].shape)
        drawn = base * np.exp(spread * noise) if base else spread * noise
        out[name] = __import__('jax').numpy.asarray(drawn.astype(out[name].dtype))
    for name, factor in factors.items():
        out[name] = (out[name] * factor).astype(out[name].dtype)
    return out
```

```python
from contextlib import ExitStack

import concourse.bass as bass
from concourse import mybir

F32 = mybir.dt.float32
I32 = mybir.dt.int32
BF16 = mybir.dt.bfloat16
ALU = mybir.AluOpType
ACT = mybir.ActivationFunctionType
AX_X = mybir.AxisListType.X

P = 128
CHUNK = 64
TOP_K = 4
EPS = 1e-6
LIMIT = 7.0
ALPHA = 1.702
GROUP = 32
GROUPS = 3
CAP = GROUP * GROUPS
STAGES = 4


def block_kernel(nc, x, attn_norm_w, w_in, gdn_conv_w, gdn_a_log, gdn_dt_bias, gdn_norm_w, cf_dw_w, cf_dw_b,
                 cf_ln_w, cf_ln_b, w_out, ffn_norm_w, w_router, b_router, w_gate_up, b_gate_up, w_down,
                 b_down, final_norm_w, out):
    _, SEQ, D = x.shape
    H = gdn_a_log.shape[1]
    DK = gdn_norm_w.shape[1]
    QK = H * DK
    CF = cf_dw_w.shape[2]
    TAPS = cf_dw_w.shape[1]
    CONV = gdn_conv_w.shape[1]
    E = w_router.shape[2]
    T = SEQ // P
    KC = D // P
    CT = CF // P
    TH = T * H
    HALF = D // 2
    QD = D // 4
    PAD = TAPS - 1
    OFF_Z = 3 * QK
    OFF_BA = OFF_Z + QK
    OFF_CF = OFF_BA + 2 * H
    SLOT = 2 * D
    NR_ROWS = SEQ + P
    ROUNDS_MAX = -(-SEQ // CAP)
    assert DK == P and H == 4 and T == 4 and KC == 8 and CT == 4 and QK == 512

    x2d = x.rearrange("b s d -> (b s) d")
    out2d = out.rearrange("b s d -> (b s) d")
    win = w_in[0].rearrange("(c p) n -> p c n", p=P)
    wout = w_out[0].rearrange("(c p) n -> p c n", p=P)

    with ExitStack() as ctx:
        def sb(name, cols, dt=F32):
            return ctx.enter_context(nc.sbuf_tensor(name, [P, cols], dt))

        def sem(name):
            return ctx.enter_context(nc.semaphore(name))

        ring = sb("ring", 8 * SLOT)
        dslots = sb("dslots", 4 * SLOT)
        rows = sb("rows", T * D)
        hbuf = sb("hbuf", T * D)
        wq = sb("wq", 8 * 512)
        qkbuf = sb("qkbuf", 2 * 2 * SEQ)
        vbuf = sb("vbuf", SEQ)
        intra = sb("intra", H * SEQ)
        zrows = sb("zrows", T * QK)
        convbuf = sb("convbuf", 2 * (SEQ + CONV - 1) + 2 * SEQ)
        sqbuf = sb("sqbuf", 2 * SEQ)
        kbg = sb("kbg", SEQ)
        ffnw = sb("ffnw", D)
        consts = sb("consts", 17 * P)
        small = sb("small", 2048)
        slot_no = sb("slot_no", GROUPS * P, BF16)
        idx = sb("idx", STAGES * GROUPS, I32)
        n_iter = sb("n_iter", 1, I32)

        def view(t, start, *dims):
            n = 1
            for d in dims:
                n *= d
            v = t[:, start:start + n]
            names = "abcd"[:len(dims)]
            if len(dims) > 1:
                v = v.rearrange(f"p ({' '.join(names)}) -> p {' '.join(names)}",
                                **{names[i]: dims[i] for i in range(1, len(dims))})
            return v

        xr = view(rows, 0, T, D)
        ktail = view(rows, 0, H, T, P)
        uval = view(rows, H * SEQ, H, T, P)
        hT = view(hbuf, 0, KC, SEQ)
        x2 = view(hbuf, 0, T, D)
        wqT = view(wq, 0, H, 2 * T, P)
        bgu_rows = wq[0:E, 0:2 * D]
        ubuf = view(dslots, 0, CT, SEQ + PAD)
        o0 = CT * (SEQ + PAD)
        cacc = view(dslots, o0, CT, SEQ)
        o0 += CT * SEQ
        Am, X, XT, Pm, DT, Dm = (view(dslots, o0 + i * SEQ, T, P) for i in range(6))
        o0 += 6 * SEQ
        assert o0 <= 4 * SLOT
        xn = view(convbuf, 0, 2, D)
        zero_rows = intra[:, 0:D]
        thbuf = convbuf[:, 2 * (SEQ + CONV - 1):]
        o0 = 2 * D
        onehot = rows[:, o0:o0 + T * GROUPS * P // 2].bitcast(BF16)
        o0 += T * GROUPS * P // 2
        tg = rows[:, o0:o0 + T * E * 3].bitcast(BF16)
        qT = [qkbuf[:, 2 * SEQ * i:2 * SEQ * i + SEQ] for i in range(2)]
        kT = [qkbuf[:, 2 * SEQ * i + SEQ:2 * SEQ * (i + 1)] for i in range(2)]
        xnT = [view(qkbuf, D * i, KC, P) for i in range(2)]
        vT = vbuf[:, :]
        intraT = view(intra, 0, H, T, P)
        zr = view(zrows, 0, T, QK)
        kbgv = view(kbg, 0, T, P)
        preb = [convbuf[:, i * (SEQ + CONV - 1):(i + 1) * (SEQ + CONV - 1)] for i in range(2)]
        th = [thbuf[:, i * SEQ:(i + 1) * SEQ] for i in range(2)]
        sq = [sqbuf[:, i * SEQ:(i + 1) * SEQ] for i in range(2)]

        (ident, ones, triu, blk, half0, half1, strict, trif) = (consts[:, i * P:(i + 1) * P] for i in range(8))
        LEVELS = [1, 2, 4, 8, 16, 32]
        lmask = {s: consts[:, (8 + i) * P:(9 + i) * P] for i, s in enumerate(LEVELS)}
        lmask1t = consts[:, 16 * P:17 * P]
        epst = consts[:, 14 * P:14 * P + 1]
        zero1 = consts[:, 14 * P + 1:14 * P + 2]
        one1 = consts[:, 14 * P + 2:14 * P + 3]
        iota_e = consts[:, 14 * P + 32:14 * P + 64]
        thr = consts[:, 14 * P + 64:14 * P + 64 + ROUNDS_MAX - 1]
        slotbase = consts[:, 15 * P:15 * P + GROUPS]
        jcol = consts[:, 15 * P + 4:15 * P + 5]
        tokp = consts[:, 15 * P + 5:15 * P + 6]

        off = [0]

        def take(*dims):
            n = 1
            for d in dims:
                n *= d
            v = view(small, off[0], *dims)
            off[0] += n
            return v

        PT = take(CT, 52)
        bgu = take(2 * KC, E)
        wab = take(KC, 2 * H)
        ssx, rstdx = take(T), take(T)
        dtb, nA, bro = take(H), take(H), take(E)
        thb, beta, betah, ya, ym, ye, yl, gg = (take(T, H) for _ in range(8))
        gc, eg, ge, kts = (take(T, H) for _ in range(4))
        gtB = take(2, TH)
        rso, rsl = take(H), take(H)
        ss2, rstd2 = take(T), take(T)
        lg = take(E)
        m8, e4, pr4, sums = take(8), take(TOP_K), take(TOP_K), take(2)
        pos = take(T, E)
        slot_gate = take(STAGES, GROUPS)
        tix = take(4, GROUPS)
        cnt = take(E)
        rnd = take(8)
        assert off[0] <= 1600, off[0]
        Gm = view(kbg, 0, T, E)
        Msk = view(kbg, T * E, T, E)
        i8 = kbg[:, 2 * T * E:2 * T * E + 8]
        gres = view(kbg, 2 * T * E + 8, T * E)
        S = view(sqbuf, 0, H, P)
        vn = view(sqbuf, SEQ, H, P)
        osb = [view(dslots, CT * (SEQ + PAD) + CT * SEQ + i * SEQ, H, P) for i in range(2)]
        osq = view(dslots, CT * (SEQ + PAD) + CT * SEQ + 2 * SEQ, H, P)
        mixT = [view(dslots, CT * (SEQ + PAD) + CT * SEQ + (3 + i) * SEQ, H, P) for i in range(2)]
        normrow = view(dslots, CT * (SEQ + PAD) + CT * SEQ + 5 * SEQ, P)
        router = take(KC, E)
        assert off[0] <= 2048, off[0]
        lgT = vbuf[:, 0:P]
        GT = vbuf[0:E, P:2 * P]
        bdn = intra[0:E, 0:D]
        ab_sb = thbuf[0:2 * H, 0:SEQ]
        prow = qkbuf[0:52, 0:CF]

        xg = view(wq, 0, GROUPS, QD)
        xT = view(wq, 768, GROUPS, 2, P)
        hid = view(wq, 1536, GROUPS, 512)
        g2 = view(wq, 3072, GROUPS, 2, P)
        sg = view(zrows, 0, GROUPS, 2, P)
        u2 = view(zrows, 768, GROUPS, 2, P)
        actT = view(intra, 1024, GROUPS, 2, P)
        yb = view(rows, 0, GROUPS, QD)
        finw = rows[:, D:2 * D]
        fin = view(hbuf, 0, T, D)

        bank = [ctx.enter_context(nc.psum_tensor(f"bank{i}", [P, 512], F32)) for i in range(8)]

        xn_dram = nc.dram_tensor("xn_rows", [NR_ROWS, D], F32, kind="Internal").ap()
        acc_dram = nc.dram_tensor("acc_rows", [NR_ROWS, D], F32, kind="Internal").ap()
        xn_q = xn_dram.rearrange("r (j n) -> (r j) n", j=4)
        acc_q = acc_dram.rearrange("r (j n) -> (r j) n", j=4)

        x_in = [sem(f"x_in{t}") for t in range(T)]
        xres_in = [sem(f"xres_in{t}") for t in range(T)]
        slot_in = [sem(f"slot_in{i}") for i in range(12)]
        param_in, gate_in, bias_in, late_in, wr_in = (sem(n) for n in
                                                      ("param_in", "gate_in", "bias_in", "late_in", "wr_in"))
        fin_in = sem("fin_in")
        zero_out, acc_out, last_out = sem("zero_out"), sem("acc_out"), sem("last_out")
        xn_out = [sem(f"xn_out{i}") for i in range(2)]
        act_self, dve_self, pool_self = sem("act_self"), sem("dve_self"), sem("pool_self")
        consts_ready, masks_ready, zeros_ready = sem("consts_ready"), sem("masks_ready"), sem("zeros_ready")
        params_turned, params_ready, bias_turned, bias_ready = (sem(n) for n in (
            "params_turned", "params_ready", "bias_turned", "bias_ready"))
        rstdx_ready, xs_ready, x_turned, h_act, h_dve = (sem(n) for n in (
            "rstdx_ready", "xs_ready", "x_turned", "h_act", "h_dve"))
        ab_done, ab_copied, ab_turned, g_ready, gsum_done, gc_ready = (sem(n) for n in (
            "ab_done", "ab_copied", "ab_turned", "g_ready", "gsum_done", "gc_ready"))
        ab_dve, ab_act, ga_ready = sem("ab_dve"), sem("ab_act"), sem("ga_ready")
        proj_done, proj_act, proj_dve = (sem(n) for n in ("proj_done", "proj_act", "proj_dve"))
        conv_ready, tanh_ready, silu_ready, sq_ready = (sem(n) for n in (
            "conv_ready", "tanh_ready", "silu_ready", "sq_ready"))
        ssum_done, rs_ready, norm_ready = sem("ssum_done"), sem("rs_ready"), sem("norm_ready")
        gcb_done, kk_done, qk_done, kv_turned = (sem(n) for n in ("gcb_done", "kk_done", "qk_done", "kv_turned"))
        diff_ready, dec_ready, dmask_ready, egb_ready = (sem(n) for n in (
            "diff_ready", "dec_ready", "dmask_ready", "egb_ready"))
        a_ready, in_ready, kv_ready, qd_ready = (sem(n) for n in ("a_ready", "in_ready", "kv_ready", "qd_ready"))
        p_done, p_ready, xx_done, xx_ready = (sem(n) for n in ("p_done", "p_ready", "xx_done", "xx_ready"))
        uw_done, uw_ready = sem("uw_done"), sem("uw_ready")
        cacc_ready, mean_done, xc_ready, csq_ready, var_done, crs_ready, cy_ready, cth_ready, cmix_ready = (
            sem(n) for n in ("cacc_ready", "mean_done", "xc_ready", "csq_ready", "var_done", "crs_ready",
                             "cy_ready", "cth_ready", "cmix_ready"))
        s_zero = sem("s_zero")
        ws_done, vn_ready, su_done, s_ready, o_done, o_copied = (sem(n) for n in (
            "ws_done", "vn_ready", "su_done", "s_ready", "o_done", "o_copied"))
        osq_ready, oss_ready, ors_ready, mix_ready, mix_turned, mixT_ready = (sem(n) for n in (
            "osq_ready", "oss_ready", "ors_ready", "mix_ready", "mix_turned", "mixT_ready"))
        zn_ready = sem("zn_ready")
        op_done, x2_ready, rstd2_ready, xn_ready, xn_turned, xnT_ready = (sem(n) for n in (
            "op_done", "x2_ready", "rstd2_ready", "xn_ready", "xn_turned", "xnT_ready"))
        lgT_done, lgT_copied, lg_done, lg_ready, mx_ready, ex_ready, gate_ready = (sem(n) for n in (
            "lgT_done", "lgT_copied", "lg_done", "lg_ready", "mx_ready", "ex_ready", "gate_ready"))
        pos_done, route_ready = sem("pos_done"), sem("route_ready")
        gt_done, gt_copied, bd_done, acc_ready = (sem(n) for n in ("gt_done", "gt_copied", "bd_done", "acc_ready"))
        hot_ready, idx_done, idx_ready, gathered, xt_done, xt_ready = (sem(n) for n in (
            "hot_ready", "idx_done", "idx_ready", "gathered", "xt_done", "xt_ready"))
        gu_used, hid_ready, ht_done, g2_ready, sg_ready, act_ready = (sem(n) for n in (
            "gu_used", "hid_ready", "ht_done", "g2_ready", "sg_ready", "act_ready"))
        d_used, y_ready, scattered = sem("d_used"), sem("y_ready"), sem("scattered")
        fss_ready, fin_ready, pool_step, landed = (sem(n) for n in ("fss_ready", "fin_ready", "pool_step",
                                                                    "landed"))

        class Own:

            def __init__(self, eng, s):
                self.eng, self.s, self.n = eng, s, 0

            def mark(self, ins):
                ins.then_inc(self.s, 1)
                self.n += 1

            def settle(self):
                self.eng.wait_ge(self.s, self.n)

        TILES = [("cf", i // 2, i % 2) for i in range(2 * CT)]
        TILES += [("qkv", i // 3, i % 3) for i in range(3 * H)]
        TILES += [("z", t, 0) for t in range(T)]
        NT = len(TILES)
        Q0 = 2 * CT
        Z0 = Q0 + 3 * H
        CF_A, CF_B = OFF_CF, OFF_CF + CF
        UNITS = [CF_A, CF_B, CF_A + 256, CF_B + 256, 0, QK, 2 * QK, 256, QK + 256, 2 * QK + 256]
        UNIT_OF = {}
        for i in range(2 * CT):
            UNIT_OF[i] = (2 * (i // 4) + i % 2, (i // 2) % 2)
        for i in range(3 * H):
            UNIT_OF[Q0 + i] = (4 + 3 * (i // 6) + i % 3, (i // 3) % 2)
        NU = len(UNITS) + 2
        LAST_TILE = {}
        for i, (u, _) in UNIT_OF.items():
            LAST_TILE[u] = max(LAST_TILE.get(u, 0), i)
        LAST_TILE[NU - 2] = LAST_TILE[NU - 1] = NT - 1
        GDN_STEPS = 16
        PER_SLOT = [5, 5, 6]

        def gdn_of(s):
            if s < Q0 + 4 or s >= Q0 + 4 + 3 * H:
                return None, []
            h, k = divmod(s - Q0 - 4, 3)
            a = sum(PER_SLOT[:k])
            return h, list(range(a, a + PER_SLOT[k]))

        def unit_ap(u):
            return view(ring, (u % 8) * SLOT, KC, 256) if u < NU - 2 else view(ring, (u % 8) * SLOT, 4, 512)

        def visits_less_two(engine):
            return engine.value_load(n_iter[0:1, 0:1], min_val=E - 2, max_val=E * ROUNDS_MAX - 2)

        def bank_of(s):
            return bank[s % 3]

        PAIRS = [(bank[0], bank[1]), (bank[2], bank[7])]

        block = ctx.enter_context(nc.Block())

        @block.sync
        def _(sp):
            for t in range(T):
                sp.dma_start(xr[:, t, :], x2d[t * P:(t + 1) * P, :]).then_inc(x_in[t], 16)
            for u in range(NU):
                if u >= 8:
                    sp.wait_ge(proj_done, LAST_TILE[u - 8] + 1)
                if u < NU - 2:
                    src = win[:, :, UNITS[u]:UNITS[u] + 256]
                else:
                    c = 4 * (u - NU + 2)
                    src = win[:, c:c + 4, OFF_Z:OFF_Z + QK]
                sp.dma_start(unit_ap(u), src).then_inc(slot_in[u % 8], 16)
            for i in range(4):
                sp.wait_ge(proj_done, LAST_TILE[4 + i] + 1)
                sp.dma_start(view(ring, (4 + i) * SLOT, 2, D), wout[:, 2 * i:2 * i + 2, :]).then_inc(
                    slot_in[4 + i], 16)

            def gate_up(i, c):
                e = i % E
                sp.dma_start(view(ring, c * SLOT, SLOT), w_gate_up[0, e, c * P:(c + 1) * P, :]).then_inc(
                    slot_in[c], 16)

            def down(i, u):
                e = i % E
                sp.dma_start(view(dslots, u * SLOT, 2, D),
                             w_down[0, e, 2 * u * P:(2 * u + 2) * P, :].rearrange("(c p) n -> p c n", p=P)
                             ).then_inc(slot_in[8 + u], 16)

            sp.wait_ge(proj_done, NT)
            for t in range(T):
                sp.dma_start(x2[:, t, :], x2d[t * P:(t + 1) * P, :]).then_inc(xres_in[t], 16)
            for c in range(KC):
                if c == 4:
                    sp.wait_ge(op_done, T)
                gate_up(0, c)
            for u in range(4):
                down(0, u)
            sp.wait_ge(route_ready, 1)
            m = visits_less_two(sp)
            for c in range(KC):
                sp.wait_ge(gu_used, c + 1)
                gate_up(1, c)
            with sp.Fori(2, m + 2) as i:
                for c in range(KC):
                    sp.wait_ge(gu_used, (i - 1) * KC + c + 1)
                    gate_up(i, c)
                for u in range(4):
                    sp.wait_ge(d_used, (i - 1) * 4 + u + 1)
                    down(i - 1, u)
            for u in range(4):
                sp.wait_ge(d_used, m * 4 + u + 5)
                down(m + 1, u)
            sp.wait_ge(scattered, m * 48 + 96)
            sp.wait_ge(acc_out, 16 * T)
            for t in range(T):
                sp.dma_start(fin[:, t, :], acc_dram[t * P:(t + 1) * P, :]).then_inc(fin_in, 16)
            for t in range(T):
                sp.wait_ge(fin_ready, t + 1)
                sp.dma_start(out2d[t * P:(t + 1) * P, :], fin[:, t, :]).then_inc(last_out, 16)
            sp.wait_ge(last_out, 16 * T)

        @block.gpsimd
        def _(pool):
            own = Own(pool, pool_self)

            def sel(v, pattern, base, ch, op=ALU.is_ge):
                own.mark(nc.gpsimd.affine_select(out=v, in_=v, compare_op=op, fill=0.0, base=base,
                                                 pattern=pattern, channel_multiplier=ch))
                own.settle()

            own.mark(nc.gpsimd.memset(consts[:, 0:14 * P], 1.0))
            own.mark(nc.gpsimd.memset(lmask1t, 1.0))
            for b in preb:
                own.mark(nc.gpsimd.memset(b[:, 0:CONV - 1], 0.0))
            own.mark(nc.gpsimd.memset(epst, EPS))
            own.mark(nc.gpsimd.memset(zero1, 0.0))
            own.mark(nc.gpsimd.memset(one1, 1.0))
            own.settle()
            nc.gpsimd.affine_select(out=ident, in_=ident, compare_op=ALU.is_equal, fill=0.0, base=0,
                                    pattern=[[-1, P]], channel_multiplier=1).then_inc(consts_ready, 1)
            nc.gpsimd.memset(zero_rows, 0.0).then_inc(zeros_ready, 1)
            pool.wait_ge(zeros_ready, 1)
            pool.dma_start(xn_dram[SEQ:NR_ROWS, :], zero_rows).then_inc(zero_out, 16)
            pool.dma_start(acc_dram[SEQ:NR_ROWS, :], zero_rows).then_inc(zero_out, 16)
            two = lambda v: v.rearrange("p (i w) -> p i w", i=2)
            sel(triu, [[1, P]], 0, -1)
            sel(two(triu), [[-CHUNK, 2], [0, CHUNK]], 0, 1)
            sel(two(blk), [[-CHUNK, 2], [0, CHUNK]], 0, 1)
            sel(two(blk), [[CHUNK, 2], [0, CHUNK]], CHUNK - 1, -1)
            sel(half0, [[0, P]], CHUNK - 1, -1)
            sel(half1, [[0, P]], -CHUNK, 1)
            sel(strict, [[-1, P]], -1, 1)
            sel(two(strict), [[CHUNK, 2], [0, CHUNK]], CHUNK - 1, -1)
            sel(trif, [[1, P]], 0, -1)
            for s in LEVELS:
                n = P // (2 * s)
                v = lmask[s].rearrange("p (i w) -> p i w", i=n)
                sel(v, [[-2 * s, n], [0, 2 * s]], 0, 1)
                sel(v, [[2 * s, n], [0, 2 * s]], s - 1, -1)
                sel(v, [[0, n], [1, 2 * s]], -s, 0)
            v = lmask1t.rearrange("p (i w) -> p i w", w=2)
            sel(v, [[2, P // 2], [0, 2]], 1, -1)
            sel(v, [[-2, P // 2], [0, 2]], -1, 1)
            sel(v, [[0, P // 2], [-1, 2]], 0, 0)
            own.mark(nc.gpsimd.iota(iota_e, pattern=[[1, E]], base=0, channel_multiplier=0,
                                    allow_small_or_imprecise_dtypes=True))
            own.mark(nc.gpsimd.iota(thr, pattern=[[CAP, ROUNDS_MAX - 1]], base=CAP, channel_multiplier=0,
                                    allow_small_or_imprecise_dtypes=True))
            own.mark(nc.gpsimd.iota(tokp, pattern=[[0, 1]], base=0, channel_multiplier=1,
                                    allow_small_or_imprecise_dtypes=True))
            own.mark(nc.gpsimd.iota(view(slot_no, 0, GROUPS, 4, GROUP),
                                    pattern=[[GROUP, GROUPS], [0, 4], [1, GROUP]], base=0, channel_multiplier=0,
                                    allow_small_or_imprecise_dtypes=True))
            for j in range(4):
                a = GROUP * j
                own.settle()
                own.mark(nc.gpsimd.iota(slotbase[a:a + GROUP, :], pattern=[[GROUP, GROUPS]], base=SEQ,
                                        channel_multiplier=1, allow_small_or_imprecise_dtypes=True))
                own.mark(nc.gpsimd.memset(jcol[a:a + GROUP, :], float(j)))
            own.settle()
            nc.gpsimd.memset(ubuf[:, :, 0:PAD], 0.0).then_inc(masks_ready, 1)

            def square(i):
                nonlocal_n = square.n
                pool.wait_ge(silu_ready, i + 1)
                if nonlocal_n >= 2:
                    pool.wait_ge(norm_ready, nonlocal_n - 1)
                h, part = divmod(i, 3)
                src = (qT if part == 0 else kT)[h % 2]
                nc.gpsimd.tensor_tensor(sq[nonlocal_n % 2], src, src, ALU.mult).then_inc(sq_ready, 1)
                square.n += 1
            square.n = 0

            def mask_decays(h):
                bc = lambda m: m.rearrange("p (o c) -> p o c", o=1).to_broadcast([P, T, P])
                pool.wait_ge(dec_ready, 2 * h + 2)
                own.mark(nc.gpsimd.tensor_tensor(Dm, Dm, bc(strict), ALU.mult))
                nc.gpsimd.tensor_tensor(DT, DT, bc(triu), ALU.mult).then_inc(dmask_ready, 1)
                own.settle()
                nc.gpsimd.tensor_tensor(Dm, Dm, beta[:, :, h:h + 1].to_broadcast([P, T, P]),
                                        ALU.mult).then_inc(dmask_ready, 1)

            pool.wait_ge(ga_ready, 1)
            for s in range(Q0, NT + 1):
                h, steps = gdn_of(s)
                if 0 in steps:
                    mask_decays(h)
                i = s - 1 - Q0
                if 0 <= i < 3 * H and i % 3 < 2:
                    square(i)
            pool.wait_ge(xc_ready, CT)
            for j in range(CT):
                nc.gpsimd.tensor_tensor(ubuf[:, j, 0:SEQ], cacc[:, j, :], cacc[:, j, :], ALU.mult).then_inc(
                    csq_ready, 1)
            for t in range(T):
                pool.wait_ge(o_copied, 2 * t + 2)
                if t >= 1:
                    pool.wait_ge(oss_ready, t)
                nc.gpsimd.tensor_tensor(osq, osb[t % 2], osb[t % 2], ALU.mult).then_inc(osq_ready, 1)

            for t in range(T):
                pool.wait_ge(xn_ready, t + 1)
                pool.dma_start(xn_dram[t * P:(t + 1) * P, :], xn[:, t % 2, :]).then_inc(xn_out[t % 2], 16)
            for i in range(2):
                pool.wait_ge(xn_out[i], 16 * T // 2)
            pool.wait_ge(zero_out, 32)

            def gather(g):
                pool.indirect_dma_start(out=xg[:, g, :], out_offset=None, in_=xn_q,
                                        in_offset=bass.IndirectOffsetOnAxis(ap=idx[:, g:g + 1], axis=0),
                                        bounds_check=None).then_inc(gathered, 16)

            def scatter(g, stage):
                c = stage * GROUPS + g
                pool.indirect_dma_start(out=acc_q,
                                        out_offset=bass.IndirectOffsetOnAxis(ap=idx[:, c:c + 1], axis=0),
                                        in_=yb[:, g, :], in_offset=None,
                                        compute_op=ALU.add).then_inc(scattered, 16)

            pool.wait_ge(idx_ready, 1)
            for g in range(GROUPS):
                gather(g)
            pool.wait_ge(idx_ready, 2)
            pool.wait_ge(xt_done, 1)
            for g in range(GROUPS):
                gather(g)
            for t in range(T):
                pool.wait_ge(acc_ready, t + 1)
                pool.dma_start(acc_dram[t * P:(t + 1) * P, :], x2[:, t, :]).then_inc(acc_out, 16)
            pool.wait_ge(acc_out, 16 * T)
            m = visits_less_two(pool)
            pool.sem_inc(landed, 1)
            with pool.Fori(1, m + 2) as i:
                pool.wait_ge(idx_ready, i + 2)
                pool.wait_ge(xt_done, i + 1)
                pool.sem_inc(pool_step, 1)
                for g in range(GROUPS):
                    gather(g)
                pool.wait_ge(y_ready, i + 1)
                pool.sem_inc(pool_step, 1)
                for g in range(GROUPS):
                    scatter(g, 3)
                pool.wait_ge(scattered, i * 48)
                pool.sem_inc(landed, 1)
            pool.wait_ge(y_ready, m + 3)
            pool.sem_inc(pool_step, 1)
            for g in range(GROUPS):
                scatter(g, 2)
            pool.wait_ge(scattered, m * 48 + 96)

        @block.scalar
        def _(act):
            own = Own(act, act_self)
            A = nc.scalar.activation
            act.dma_start(prow[0:TAPS, :], cf_dw_w[0]).then_inc(param_in, 16)
            for i, v in enumerate((cf_dw_b, cf_ln_w, cf_ln_b)):
                act.dma_start(prow[TAPS + i:TAPS + i + 1, :], v).then_inc(param_in, 16)
            act.dma_start(prow[34:46, :], gdn_conv_w[0].rearrange("w (s c) -> (w s) c", s=3)).then_inc(
                param_in, 16)
            act.dma_start(prow[46:48, :], attn_norm_w.rearrange("o (r c) -> (o r) c", r=2)).then_inc(
                param_in, 16)
            act.dma_start(bgu_rows, b_gate_up[0]).then_inc(bias_in, 16)
            act.dma_start(wab, win[:, :, OFF_BA:OFF_BA + 2 * H]).then_inc(gate_in, 16)
            act.dma_start(dtb, gdn_dt_bias[0:1, :].to_broadcast([P, H])).then_inc(gate_in, 16)
            act.dma_start(nA, gdn_a_log[0:1, :].to_broadcast([P, H])).then_inc(gate_in, 16)
            act.dma_start(router, w_router[0].rearrange("(c p) e -> p c e", p=P)).then_inc(wr_in, 16)
            act.dma_start(bro, b_router[0:1, :].to_broadcast([P, E])).then_inc(wr_in, 16)
            act.dma_start(ffnw[:, :], ffn_norm_w[0:1, :].to_broadcast([P, D])).then_inc(wr_in, 16)

            act.wait_ge(consts_ready, 1)
            for t in range(T):
                act.wait_ge(x_in[t], 16)
                own.mark(A(zrows[:, (t % 2) * D:(t % 2) * D + D], xr[:, t, :], ACT.Square,
                           accum_out=ssx[:, t:t + 1]))
                own.settle()
                own.mark(A(rstdx[:, t:t + 1], ssx[:, t:t + 1], ACT.Ln, bias=epst, scale=1.0 / D))
                own.settle()
                A(rstdx[:, t:t + 1], rstdx[:, t:t + 1], ACT.Exp, scale=-0.5).then_inc(rstdx_ready, 1)
            act.wait_ge(bias_turned, 1)
            A(bgu.rearrange("p a b -> p (a b)"), bank[4][:, :], ACT.Copy).then_inc(bias_ready, 1)
            act.wait_ge(params_ready, 1)
            for c in range(0, KC, 2):
                act.wait_ge(x_turned, c + 1)
                A(hT[:, c, :], bank[c][:, :], ACT.Copy, scale=PT[:, c % CT, 46 + c // CT:47 + c // CT]
                  ).then_inc(h_act, 1)
            act.wait_ge(ab_done, 1)
            A(ab_sb, bank[3][0:2 * H, :], ACT.Copy).then_inc(ab_copied, 1)
            act.wait_ge(ab_turned, 1)
            act.wait_ge(gate_in, 48)
            act.wait_ge(ab_dve, 1)
            A(thb, view(bank[4], 0, T, 2 * H)[:, :, 0:H], ACT.Tanh, scale=0.5).then_inc(ab_act, 1)
            own.mark(A(nA, nA, ACT.Exp))
            own.mark(A(ye, ya, ACT.Exp, scale=-1.0))
            own.settle()
            A(yl, ye, ACT.Ln, bias=one1).then_inc(ab_act, 1)
            act.wait_ge(gsum_done, 1)
            act.wait_ge(gc_ready, 1)
            own.mark(A(eg, gc, ACT.Exp))
            own.mark(A(kts, kts, ACT.Exp))
            A(gtB, view(bank[4], 128, 2, TH), ACT.Exp).then_inc(ab_act, 1)

            def tile_copy(s):
                kind, a, b = TILES[s]
                if kind == "cf":
                    if b == 1:
                        act.wait_ge(proj_done, s + 1)
                        if a >= 2:
                            act.wait_ge(proj_dve, a - 1)
                        if a == 0:
                            act.wait_ge(ab_turned, 1)
                        A(th[a % 2], bank_of(s)[:, :], ACT.Tanh, scale=0.5).then_inc(proj_act, 1)
                elif kind == "qkv":
                    i = 3 * a + b
                    act.wait_ge(proj_done, s + 1)
                    if i >= 2:
                        act.wait_ge(conv_ready, i - 1)
                    A(preb[i % 2][:, CONV - 1:], bank_of(s)[:, :], ACT.Copy).then_inc(proj_act, 1)
                else:
                    act.wait_ge(proj_done, s + 1)
                    act.wait_ge(silu_ready, 3 * H)
                    if a >= 1:
                        act.wait_ge(proj_dve, CT + a)
                    A(th[1], bank_of(s)[:, :], ACT.Tanh, scale=0.5).then_inc(proj_act, 1)

            def tile_tanh(s):
                kind, a, b = TILES[s]
                if kind != "qkv":
                    return
                i = 3 * a + b
                act.wait_ge(conv_ready, i + 1)
                dst = (qT[a % 2], kT[a % 2], vT)[b]
                if i >= 1:
                    act.wait_ge(silu_ready, i)
                if i == 0:
                    act.wait_ge(proj_dve, CT)
                A(th[1], dst, ACT.Tanh, scale=0.5).then_inc(tanh_ready, 1)

            def tile_rs(s):
                kind, a, b = TILES[s]
                if kind != "qkv" or b == 2:
                    return
                n = 2 * a + b
                act.wait_ge(ssum_done, n + 1)
                v = sq[n % 2]
                own.mark(A(v, bank[3 + b][:, :], ACT.Ln, bias=epst, scale=0.25))
                own.settle()
                A(v, v, ACT.Exp, scale=-0.5).then_inc(rs_ready, 1)

            def gdn(h, k):
                if k == 0:
                    act.wait_ge(gcb_done, h + 1)
                    if h >= 1:
                        act.wait_ge(qd_ready, h)
                    act.wait_ge(diff_ready, h + 1)
                    A(Dm, Dm, ACT.Exp).then_inc(dec_ready, 1)
                    A(DT, DT, ACT.Exp).then_inc(dec_ready, 1)
                    A(th[0], bank[7][:, :], ACT.Exp).then_inc(egb_ready, 1)
                if k == GDN_STEPS - 1:
                    act.wait_ge(uw_done, h + 1)
                    A(uval[:, h, :, :], view(bank[3], 0, T, P), ACT.Copy).then_inc(uw_ready, 1)
                    w = view(bank[4], 0, T, 2, CHUNK)
                    d = wqT[:, h, :, :].rearrange("p (t f) c -> p t f c", f=2)
                    A(d[:, :, 0, 0:CHUNK], w[:, :, 0, :], ACT.Copy).then_inc(uw_ready, 1)
                    A(d[:, :, 1, CHUNK:P], w[:, :, 1, :], ACT.Copy).then_inc(uw_ready, 1)

            for s in range(NT + 1):
                h, steps = gdn_of(s)
                if 0 in steps:
                    gdn(h, 0)
                if s >= 1:
                    tile_copy(s - 1)
                    tile_tanh(s - 1)
                if s >= 2:
                    tile_rs(s - 2)
                if GDN_STEPS - 1 in steps:
                    gdn(h, GDN_STEPS - 1)
            act.wait_ge(a_ready, H)
            act.dma_start(normrow, gdn_norm_w[0:1, :].to_broadcast([P, P])).then_inc(late_in, 16)
            act.wait_ge(var_done, 1)
            act.wait_ge(kv_ready, H)
            crs = vbuf[:, :]
            own.mark(A(crs, bank[0][:, :], ACT.Ln, bias=epst, scale=1.0 / CF))
            own.settle()
            A(crs, crs, ACT.Exp, scale=-0.5).then_inc(crs_ready, 1)

            def o_copy(n):
                t, f = divmod(n, 2)
                ob, b = (CHUNK, 0) if f == 0 else (0, CHUNK)
                act.wait_ge(o_done, n + 1)
                if t >= 2:
                    act.wait_ge(mix_turned, t - 1)
                A(osb[t % 2][b:b + CHUNK, :, :], view(bank[3 + n % 2], 0, H, P)[ob:ob + CHUNK, :, :],
                  ACT.Copy).then_inc(o_copied, 1)

            def o_rstd(t):
                act.wait_ge(oss_ready, t + 1)
                if t >= 1:
                    act.wait_ge(mix_ready, t)
                own.mark(A(rsl, rso, ACT.Ln, bias=epst, scale=1.0 / DK))
                own.settle()
                A(rsl, rsl, ACT.Exp, scale=-0.5).then_inc(ors_ready, 1)

            def mixT_copy(t):
                act.wait_ge(mix_turned, t + 1)
                if t >= 2:
                    act.wait_ge(op_done, t - 1)
                A(mixT[t % 2], view(bank[6], 0, H, P), ACT.Copy).then_inc(mixT_ready, 1)

            def x2_rstd(t):
                act.wait_ge(x2_ready, t + 1)
                own.mark(A(zrows[:, 0:D], x2[:, t, :], ACT.Square, accum_out=ss2[:, t:t + 1]))
                own.settle()
                own.mark(A(rstd2[:, t:t + 1], ss2[:, t:t + 1], ACT.Ln, bias=epst, scale=1.0 / D))
                own.settle()
                A(rstd2[:, t:t + 1], rstd2[:, t:t + 1], ACT.Exp, scale=-0.5).then_inc(rstd2_ready, 1)

            def xnT_copy(t):
                act.wait_ge(xn_turned, t + 1)
                if t >= 2:
                    act.wait_ge(lgT_done, t - 1)
                own.mark(A(xnT[t % 2][:, 0:4, :], view(bank[3], 0, 4, P), ACT.Copy))
                own.mark(A(xnT[t % 2][:, 4:8, :], view(bank[4], 0, 4, P), ACT.Copy))
                own.settle()
                act.sem_inc(xnT_ready, 1)

            def lgT_copy(t):
                act.wait_ge(lgT_done, t + 1)
                if t >= 1:
                    act.wait_ge(lg_done, t)
                A(lgT, bank[5][:, 0:P], ACT.Copy).then_inc(lgT_copied, 1)

            def top_exp(t):
                act.wait_ge(mx_ready, t + 1)
                A(e4, e4, ACT.Exp, accum_out=sums[:, 0:1]).then_inc(ex_ready, 1)

            for n in range(2 * T):
                o_copy(n)
                if n == 1:
                    for j in range(CT):
                        act.wait_ge(cy_ready, j + 1)
                        A(ubuf[:, j, 0:SEQ], cacc[:, j, :], ACT.Tanh).then_inc(cth_ready, 1)
                if n == 3:
                    mixT_copy(0)
                if n == 5:
                    mixT_copy(1)
                if n % 2 == 1:
                    o_rstd(n // 2)
            act.dma_start(bdn, b_down[0]).then_inc(bias_in, 16)
            act.wait_ge(mix_ready, T)
            x2_rstd(0)
            mixT_copy(2)
            x2_rstd(1)
            xnT_copy(0)
            lgT_copy(0)
            mixT_copy(3)
            for t in range(1, T):
                xnT_copy(t)
                lgT_copy(t)
                top_exp(t - 1)
                if t + 1 < T:
                    x2_rstd(t + 1)
            top_exp(T - 1)

            def gt_copy(t):
                act.wait_ge(gt_done, t + 1)
                if t >= 1:
                    act.wait_ge(bd_done, t)
                A(GT, bank[2][0:E, 0:P], ACT.Copy).then_inc(gt_copied, 1)

            def xT_copy(v):
                act.wait_ge(xt_done, v)
                own.mark(A(xT[:, 0:2, :, :], view(bank[5], 0, 2, 2, P), ACT.Copy))
                own.mark(A(xT[:, 2, :, :], view(bank[6], 0, 2, P), ACT.Copy))

            xT_copy(1)
            own.settle()
            act.sem_inc(xt_ready, 1)
            for t in range(T):
                gt_copy(t)
            m = visits_less_two(act)

            def hid_copy():
                for g in range(GROUPS):
                    A(hid[:, g, :], bank[g][:, :], ACT.Copy).then_inc(hid_ready, 1)

            def xT_copy_loop(v):
                act.wait_ge(xt_done, v)
                A(xT[:, 0:2, :, :], view(bank[5], 0, 2, 2, P), ACT.Copy).then_inc(xt_ready, 1)
                A(xT[:, 2, :, :], view(bank[6], 0, 2, P), ACT.Copy).then_inc(xt_ready, 1)

            def results(stage):
                A(yb[:, 0, :], bank[3][:, 0:QD], ACT.Copy, scale=slot_gate[:, stage, 0:1])
                A(yb[:, 1, :], bank[3][:, QD:2 * QD], ACT.Copy, scale=slot_gate[:, stage, 1:2])
                A(yb[:, 2, :], bank[4][:, 0:QD], ACT.Copy, scale=slot_gate[:, stage, 2:3]).then_inc(y_ready, 1)

            act.sem_inc(y_ready, 1)
            act.wait_ge(gu_used, KC)
            hid_copy()
            xT_copy_loop(2)
            with act.Fori(1, m + 2) as i:
                act.wait_ge(g2_ready, i)
                A(sg, g2, ACT.Sigmoid, scale=ALPHA).then_inc(sg_ready, 1)
                act.wait_ge(gu_used, i * KC + KC)
                hid_copy()
                xT_copy_loop(i + 2)
                act.wait_ge(d_used, i * 4 + 4)
                act.wait_ge(idx_ready, i + 3)
                act.wait_ge(landed, i)
                results(3)
            act.wait_ge(g2_ready, m + 2)
            A(sg, g2, ACT.Sigmoid, scale=ALPHA).then_inc(sg_ready, 1)
            act.wait_ge(d_used, m * 4 + 12)
            act.wait_ge(landed, m + 2)
            results(2)
            act.dma_start(finw, final_norm_w.rearrange("(o d) -> o d", o=1).to_broadcast([P, D])).then_inc(
                late_in, 16)
            for t in range(T):
                act.wait_ge(fin_in, 16 * T)
                A(ring[:, t * D:(t + 1) * D], fin[:, t, :], ACT.Square, accum_out=ssx[:, t:t + 1]).then_inc(
                    fss_ready, 1)
            act.wait_ge(fss_ready, T)
            A(ssx, ssx, ACT.Ln, bias=epst, scale=1.0 / D).then_inc(fss_ready, 1)
            act.wait_ge(fss_ready, T + 1)
            A(rstdx, ssx, ACT.Exp, scale=-0.5).then_inc(fss_ready, 1)

        @block.vector
        def _(dve):
            own = Own(dve, dve_self)
            V = nc.vector
            bcm = lambda m: m.rearrange("p (o c) -> p o c", o=1).to_broadcast([P, T, P])

            dve.wait_ge(params_turned, 1)
            own.mark(V.tensor_copy(PT[:, :, 0:48], view(bank[3], 0, CT, 64)[:, :, 0:48]))
            own.settle()
            own.mark(V.tensor_scalar(PT[:, :, 0:TAPS], PT[:, :, 0:TAPS], 0.5, None, ALU.mult))
            own.mark(V.tensor_scalar(PT[:, :, 32:34], PT[:, :, 32:34], 0.5, None, ALU.mult))
            own.settle()
            dve.sem_inc(params_ready, 1)
            for t in range(T):
                dve.wait_ge(rstdx_ready, t + 1)
                V.tensor_scalar(xr[:, t, :], xr[:, t, :], rstdx[:, t:t + 1], None, ALU.mult).then_inc(xs_ready, 1)
            for c in range(1, KC, 2):
                dve.wait_ge(x_turned, c + 1)
                V.tensor_scalar(hT[:, c, :], bank[c][:, :], PT[:, c % CT, 46 + c // CT:47 + c // CT], None,
                                ALU.mult).then_inc(h_dve, 1)
            dve.wait_ge(ab_turned, 1)
            dve.wait_ge(gate_in, 48)
            own.mark(V.tensor_tensor(ym, view(bank[4], 0, T, 2 * H)[:, :, H:2 * H],
                                     dtb.rearrange("p (o h) -> p o h", o=1).to_broadcast([P, T, H]), ALU.add))
            own.settle()
            V.scalar_tensor_tensor(out=ya, in0=ym, scalar=-1.0, in1=ym, op0=ALU.mult, op1=ALU.max
                                   ).then_inc(ab_dve, 1)
            dve.wait_ge(ab_act, 1)
            own.mark(V.tensor_scalar(beta, thb, 0.5, 0.5, ALU.mult, ALU.add))
            own.mark(V.tensor_scalar(ym, ym, 0.0, None, ALU.max))
            own.settle()
            own.mark(V.tensor_scalar(betah, beta, 0.5, None, ALU.mult))
            dve.wait_ge(ab_act, 2)
            own.mark(V.tensor_tensor(ym, ym, yl, ALU.add))
            own.settle()
            V.scalar_tensor_tensor(out=gg, in0=ym, scalar=-1.0,
                                   in1=nA.rearrange("p (o h) -> p o h", o=1).to_broadcast([P, T, H]),
                                   op0=ALU.mult, op1=ALU.mult).then_inc(g_ready, 1)
            dve.wait_ge(gsum_done, 1)
            own.mark(V.tensor_copy(gc, view(bank[4], 64, T, H)))
            own.settle()
            own.mark(V.tensor_tensor(kts, view(bank[4], 96, T, H), gc, ALU.subtract))
            own.settle()
            dve.sem_inc(gc_ready, 1)
            dve.wait_ge(ab_act, 3)
            V.tensor_tensor(ge, beta, eg, ALU.mult).then_inc(ga_ready, 1)

            def cf_value(j):
                dve.wait_ge(proj_act, j + 1)
                V.scalar_tensor_tensor(out=ubuf[:, j, PAD:], in0=th[j % 2], scalar=1.0,
                                       in1=bank_of(2 * j)[:, :], op0=ALU.add, op1=ALU.mult
                                       ).then_inc(proj_dve, 1)

            tap_at = [0]

            def taps(n, j_max):
                for _ in range(n):
                    j, k = divmod(tap_at[0], TAPS)
                    if j > j_max or j >= CT:
                        return
                    if k == 0:
                        dve.wait_ge(proj_dve, j + 1)
                        own.mark(V.tensor_scalar(cacc[:, j, :], ubuf[:, j, 0:SEQ], PT[:, j, 0:1],
                                                 PT[:, j, TAPS:TAPS + 1], ALU.mult, ALU.add))
                    else:
                        own.settle()
                        own.mark(V.scalar_tensor_tensor(out=cacc[:, j, :], in0=ubuf[:, j, k:k + SEQ],
                                                        scalar=PT[:, j, k:k + 1], in1=cacc[:, j, :],
                                                        op0=ALU.mult, op1=ALU.add))
                    tap_at[0] += 1
                    if k == TAPS - 1:
                        own.settle()
                        dve.sem_inc(cacc_ready, 1)

            def conv4(s):
                kind, h, b = TILES[s]
                if kind != "qkv":
                    return
                i = 3 * h + b
                dst = (qT[h % 2], kT[h % 2], vT)[b]
                dve.wait_ge(proj_act, CT + i + 1)
                if b < 2 and h >= 2:
                    dve.wait_ge(qk_done, h - 1)
                    dve.wait_ge(kv_turned, h - 1)
                if b == 2 and h >= 1:
                    dve.wait_ge(kv_turned, h)
                w = lambda k: PT[:, h, 34 + 3 * k + b:35 + 3 * k + b]
                own.mark(V.tensor_scalar(dst, preb[i % 2][:, 0:SEQ], w(0), None, ALU.mult))
                for k in range(1, CONV):
                    own.settle()
                    ins = V.scalar_tensor_tensor(out=dst, in0=preb[i % 2][:, k:k + SEQ], scalar=w(k), in1=dst,
                                                 op0=ALU.mult, op1=ALU.add)
                    if k < CONV - 1:
                        own.mark(ins)
                ins.then_inc(conv_ready, 1)

            def silu(s):
                kind, h, b = TILES[s]
                if kind == "z":
                    dve.wait_ge(proj_act, CT + 3 * H + h + 1)
                    V.scalar_tensor_tensor(out=zr[:, h, :], in0=th[1], scalar=1.0, in1=bank_of(s)[:, :],
                                           op0=ALU.add, op1=ALU.mult).then_inc(proj_dve, 1)
                if kind != "qkv":
                    return
                i = 3 * h + b
                dst = (qT[h % 2], kT[h % 2], vT)[b]
                dve.wait_ge(tanh_ready, i + 1)
                V.scalar_tensor_tensor(out=dst, in0=th[1], scalar=1.0, in1=dst, op0=ALU.add,
                                       op1=ALU.mult).then_inc(silu_ready, 1)

            def norm(s):
                kind, h, b = TILES[s]
                if kind != "qkv" or b == 2:
                    return
                dst = (qT[h % 2], kT[h % 2])[b]
                dve.wait_ge(rs_ready, 2 * h + b + 1)
                V.scalar_tensor_tensor(out=dst, in0=dst, scalar=0.5 * (DK ** -0.5 if b == 0 else 1.0),
                                       in1=sq[b], op0=ALU.mult, op1=ALU.mult).then_inc(norm_ready, 1)

            def level(h, s):
                if s == 1:
                    dve.wait_ge(p_done, 6 * h + 1)
                    own.mark(V.tensor_tensor(Pm, view(bank[5], 0, T, P), bcm(lmask[1]), ALU.mult))
                    own.settle()
                    V.scalar_tensor_tensor(out=XT, in0=Pm, scalar=-1.0, in1=bcm(ident), op0=ALU.mult,
                                           op1=ALU.add).then_inc(xx_ready, 1)
                    return
                dve.wait_ge(p_done, 6 * h + LEVELS.index(s) + 1)
                V.tensor_tensor(Pm, view(bank[5], 0, T, P), bcm(lmask[s]), ALU.mult).then_inc(p_ready, 1)

            def level_x(h, s):
                k = LEVELS.index(s)
                dve.wait_ge(xx_done, 5 * h + k)
                V.tensor_tensor(XT, XT, view(bank[7], 0, T, P), ALU.subtract).then_inc(xx_ready, 1)
                if s < LEVELS[-1]:
                    V.tensor_tensor(X, X, view(bank[6], 0, T, P), ALU.subtract).then_inc(xx_ready, 1)

            def gdn(h, k):
                if k == 0:
                    dve.wait_ge(gcb_done, h + 1)
                    if h >= 1:
                        dve.wait_ge(uw_done, h)
                    own.mark(V.tensor_tensor(DT, view(bank[7], 0, T, P),
                                             gc[:, :, h:h + 1].to_broadcast([P, T, P]), ALU.subtract))
                    own.settle()
                    own.mark(V.tensor_scalar(Dm, DT, -1.0, 0.0, ALU.mult, ALU.min))
                    own.settle()
                    own.mark(V.tensor_scalar(DT, DT, 0.0, None, ALU.min))
                    own.settle()
                    dve.sem_inc(diff_ready, 1)
                if k == 1:
                    dve.wait_ge(egb_ready, h + 1)
                    if h == 0:
                        dve.wait_ge(bias_ready, 1)
                    q = qT[h % 2].rearrange("p (t f c) -> p t f c", t=T, f=2)
                    e = th[0].rearrange("p (t f c) -> p t f c", t=T, f=2)
                    d = wqT[:, h, :, :].rearrange("p (t f) c -> p t f c", f=2)
                    own.mark(V.tensor_tensor(d[:, :, 0, CHUNK:P], q[:, :, 0, :], e[:, :, 0, :], ALU.mult))
                    own.mark(V.tensor_tensor(d[:, :, 1, 0:CHUNK], q[:, :, 1, :], e[:, :, 1, :], ALU.mult))
                    own.settle()
                    dve.sem_inc(qd_ready, 1)
                if k == 2:
                    dve.wait_ge(dmask_ready, 2 * h + 2)
                    dve.wait_ge(kk_done, h + 1)
                    V.tensor_tensor(Am, view(bank[5], 0, T, P), Dm, ALU.mult).then_inc(a_ready, 1)
                    dve.wait_ge(qk_done, h + 1)
                    if h == 0:
                        dve.wait_ge(zero_out, 32)
                    V.tensor_tensor(intraT[:, h, :, :], view(bank[6], 0, T, P), DT, ALU.mult
                                    ).then_inc(in_ready, 1)
                    dve.wait_ge(a_ready, h + 1)
                    own.mark(V.tensor_tensor(X, Am, bcm(lmask1t), ALU.mult))
                    own.settle()
                    V.scalar_tensor_tensor(out=X, in0=X, scalar=-1.0, in1=bcm(ident), op0=ALU.mult,
                                           op1=ALU.add).then_inc(xx_ready, 1)
                if k == 3:
                    dve.wait_ge(kv_turned, h + 1)
                    bct = lambda v: v[:, :, h:h + 1].to_broadcast([P, T, P])
                    own.mark(V.tensor_tensor(kbgv, view(bank[3], 0, T, P), bct(ge), ALU.mult))
                    own.mark(V.tensor_tensor(ktail[:, h, :, :], view(bank[3], 0, T, P), bct(kts), ALU.mult))
                    own.mark(V.tensor_tensor(uval[:, h, :, :], view(bank[4], 0, T, P), bct(betah), ALU.mult))
                    own.settle()
                    dve.sem_inc(kv_ready, 1)
                if k == 4:
                    level(h, 1)
                if 5 <= k < 15:
                    s = LEVELS[1 + (k - 5) // 2]
                    if k % 2 == 1:
                        level(h, s)
                    else:
                        level_x(h, s)

            dve.wait_ge(masks_ready, 1)
            for s in range(NT + 1):
                h, steps = gdn_of(s)
                p = s - 1
                if 1 <= s <= 2 * CT and s % 2 == 0:
                    cf_value(s // 2 - 1)
                jobs = []
                if p >= 0:
                    jobs += [lambda: conv4(p), lambda: silu(p)]
                if s >= 2:
                    jobs.insert(1, lambda: norm(s - 2))
                quota = 7 if 2 <= s < Q0 + 4 else 5
                if s >= 2:
                    jobs.append(lambda: taps(quota, CT - 1 if s >= Q0 else (s - 2) // 2))
                for n in range(max(len(steps), len(jobs))):
                    if n < len(steps):
                        gdn(h, steps[n])
                    if n < len(jobs):
                        jobs[n]()
            while tap_at[0] < CT * TAPS:
                taps(1, CT)
            dve.wait_ge(mean_done, 1)
            for j in range(CT):
                V.scalar_tensor_tensor(out=cacc[:, j, :], in0=bank[1][:, :], scalar=-1.0 / CF,
                                       in1=cacc[:, j, :], op0=ALU.mult, op1=ALU.add).then_inc(xc_ready, 1)
            own.mark(V.memset(S, 0.0))
            own.settle()
            dve.sem_inc(s_zero, 1)

            def conf_scale():
                dve.wait_ge(crs_ready, 1)
                for j in range(CT):
                    dve.wait_ge(csq_ready, j + 1)
                    own.mark(V.tensor_tensor(cacc[:, j, :], cacc[:, j, :], vbuf[:, :], ALU.mult))

            def conf_affine():
                for j in range(CT):
                    own.settle()
                    V.tensor_scalar(cacc[:, j, :], cacc[:, j, :], PT[:, j, 32:33], PT[:, j, 33:34], ALU.mult,
                                    ALU.add).then_inc(cy_ready, 1)

            def conf_silu():
                for j in range(CT):
                    dve.wait_ge(cth_ready, j + 1)
                    V.scalar_tensor_tensor(out=cacc[:, j, :], in0=ubuf[:, j, 0:SEQ], scalar=1.0,
                                           in1=cacc[:, j, :], op0=ALU.add, op1=ALU.mult).then_inc(cmix_ready, 1)

            def z_weight():
                dve.wait_ge(late_in, 16)
                dve.wait_ge(proj_dve, CT + T)
                for t in range(T):
                    zt = zr[:, t, :].rearrange("p (h c) -> p h c", h=H)
                    own.mark(V.scalar_tensor_tensor(
                        out=zt, in0=zt, scalar=0.5,
                        in1=normrow.rearrange("p (o c) -> p o c", o=1).to_broadcast([P, H, P]),
                        op0=ALU.mult, op1=ALU.mult))

            def rec(n):
                t, f = divmod(n, 2)
                b = CHUNK * f
                dve.wait_ge(ws_done, n + 1)
                V.tensor_tensor(vn[b:b + CHUNK, :, :], uval[b:b + CHUNK, :, t, :],
                                view(bank[3 + n % 2], 0, H, P)[b:b + CHUNK, :, :], ALU.subtract
                                ).then_inc(vn_ready, 1)
                dve.wait_ge(su_done, n + 1)
                for h in range(H):
                    V.scalar_tensor_tensor(out=S[:, h, :], in0=S[:, h, :],
                                           scalar=gtB[:, f, t * H + h:t * H + h + 1],
                                           in1=view(bank[5], 0, H, P)[:, h, :], op0=ALU.mult,
                                           op1=ALU.add).then_inc(s_ready, 1)

            def gated(t):
                dve.wait_ge(osq_ready, t + 1)
                V.tensor_reduce(rso, osq, AX_X, ALU.add).then_inc(oss_ready, 1)
                dve.wait_ge(ors_ready, t + 1)
                o = osb[t % 2]
                own.mark(V.tensor_tensor(o, o, rsl.rearrange("p (h o) -> p h o", o=1).to_broadcast([P, H, P]),
                                         ALU.mult))
                own.settle()
                V.tensor_tensor(o, o, zr[:, t, :].rearrange("p (h c) -> p h c", h=H), ALU.mult
                                ).then_inc(mix_ready, 1)

            def residual(t):
                pair = PAIRS[t % 2]
                dve.wait_ge(op_done, t + 1)
                dve.wait_ge(xres_in[t], 16)
                own.mark(V.tensor_tensor(x2[:, t, 0:HALF], pair[0][:, :], x2[:, t, 0:HALF], ALU.add))
                own.mark(V.tensor_tensor(x2[:, t, HALF:D], pair[1][:, :], x2[:, t, HALF:D], ALU.add))
                own.settle()
                dve.sem_inc(x2_ready, 1)

            def normed(t):
                dve.wait_ge(rstd2_ready, t + 1)
                if t >= 2:
                    dve.wait_ge(xn_turned, t - 1)
                    dve.wait_ge(xn_out[t % 2], 16 * (t // 2))
                if t == 0:
                    dve.wait_ge(zero_out, 32)
                    dve.wait_ge(wr_in, 48)
                V.scalar_tensor_tensor(out=xn[:, t % 2, :], in0=x2[:, t, :], scalar=rstd2[:, t:t + 1],
                                       in1=ffnw[:, :], op0=ALU.mult, op1=ALU.mult).then_inc(xn_ready, 1)

            def route(t):
                dve.wait_ge(lg_done, t + 1)
                own.mark(V.tensor_reduce(lg, bank[6][:, 0:P].rearrange("p (j e) -> p e j", j=4), AX_X,
                                         ALU.add))
                own.settle()
                own.mark(V.tensor_tensor(lg, lg, bro, ALU.add))
                own.settle()
                own.mark(V.max(m8, lg))
                own.settle()
                own.mark(V.max_index(i8.bitcast(mybir.dt.uint32), m8, lg))
                own.mark(V.tensor_scalar(e4, m8[:, 0:TOP_K], m8[:, 0:1], None, ALU.subtract))
                own.settle()
                dve.sem_inc(mx_ready, 1)
                own.mark(V.tensor_copy(pr4, i8.bitcast(mybir.dt.uint32)[:, 0:TOP_K]))
                dve.wait_ge(ex_ready, t + 1)
                own.mark(V.reciprocal(sums[:, 1:2], sums[:, 0:1]))
                own.settle()
                own.mark(V.tensor_scalar(e4, e4, sums[:, 1:2], None, ALU.mult))
                own.settle()
                own.mark(V.tensor_scalar(Gm[:, t, :], iota_e, pr4[:, 0:1], e4[:, 0:1], ALU.is_equal, ALU.mult))
                for k in range(1, TOP_K):
                    own.mark(V.tensor_scalar(lg, iota_e, pr4[:, k:k + 1], e4[:, k:k + 1], ALU.is_equal,
                                             ALU.mult))
                    own.settle()
                    own.mark(V.tensor_tensor(Gm[:, t, :], Gm[:, t, :], lg, ALU.add))
                    own.settle()
                V.tensor_scalar(Msk[:, t, :], Gm[:, t, :], 0.0, None, ALU.is_gt).then_inc(gate_ready, 1)

            rec(0)
            conf_scale()
            rec(1)
            conf_affine()
            z_weight()
            rec(2)
            gated(0)
            conf_silu()
            rec(3)
            rec(4)
            gated(1)
            rec(5)
            rec(6)
            gated(2)
            rec(7)
            residual(0)
            gated(3)
            normed(0)
            residual(1)
            normed(1)
            route(0)
            residual(2)
            normed(2)
            route(1)
            residual(3)
            normed(3)
            route(2)
            route(3)
            tgv = view(tg, 0, T * E, 6)
            for t in range(T):
                own.mark(V.memset(tgv[:, t * E:(t + 1) * E, 0:1], float(t * P)))
            own.mark(V.tensor_copy(tgv[:, :, 1:2], tokp.rearrange("p (a b) -> p a b", a=1).to_broadcast(
                [P, T * E, 1])))
            own.mark(V.memset(tgv[:, :, 2:3], 1.0))
            gflat = view(kbg, 0, T * E, 1)
            gr = view(kbg, 2 * T * E + 8, T * E, 1)
            own.mark(V.tensor_copy(tgv[:, :, 3:4], gflat))
            own.settle()
            own.mark(V.tensor_tensor(gr, gflat, tgv[:, :, 3:4], ALU.subtract))
            own.settle()
            own.mark(V.tensor_copy(tgv[:, :, 4:5], gr))
            own.settle()
            own.mark(V.tensor_tensor(gr, gr, tgv[:, :, 4:5], ALU.subtract))
            own.settle()
            own.mark(V.tensor_copy(tgv[:, :, 5:6], gr))
            dve.wait_ge(pos_done, 1)
            pv = view(bank[6], 0, T, E)
            own.mark(V.tensor_tensor(pos, Msk, pv, ALU.mult))
            own.mark(V.tensor_reduce(rnd[:, 0:1], bank[6][:, T * E:T * E + E], AX_X, ALU.max))
            own.settle()
            own.mark(V.tensor_scalar(pos, pos, -1.0, None, ALU.add))
            own.mark(V.tensor_scalar(rnd[:, 1:1 + ROUNDS_MAX - 1], thr, rnd[:, 0:1], None, ALU.is_lt))
            own.settle()
            own.mark(V.tensor_reduce(rnd[:, 7:8], rnd[:, 1:1 + ROUNDS_MAX - 1], AX_X, ALU.add))
            own.settle()
            own.mark(V.tensor_scalar(n_iter[:, 0:1], rnd[:, 7:8], float(E), float(E - 2), ALU.mult, ALU.add))
            own.settle()
            dve.sem_inc(route_ready, 1)

            ohv = view(onehot, 0, T, GROUPS * P)

            def hot(e):
                for t in range(T):
                    V.tensor_scalar(ohv[:, t, :], slot_no[:, :], pos[:, t, bass.ds(e, 1)], None,
                                    ALU.is_equal).then_inc(hot_ready, 1)

            def lower(e):
                V.tensor_scalar(pos[:, :, bass.ds(e, 1)], pos[:, :, bass.ds(e, 1)], float(-CAP), None,
                                ALU.add).then_inc(hot_ready, 1)

            iv = idx[:, :].rearrange("p (s g) -> p s g", s=STAGES)
            STEPS_IDX = 13

            def numbers(base):
                ps = bank[7][:, 0:GROUPS * 6].rearrange("p (g c) -> p g c", c=6)
                s = own.s
                c = base

                def mk(ins):
                    nonlocal c
                    ins.then_inc(s, 1)
                    c = c + 1

                for k in range(STAGES - 1, 0, -1):
                    mk(V.tensor_copy(iv[:, k, :], iv[:, k - 1, :]))
                    mk(V.tensor_copy(slot_gate[:, k, :], slot_gate[:, k - 1, :]))
                    if k > 1:
                        dve.wait_ge(s, c)
                mk(V.tensor_tensor(tix[:, 0, :], slotbase, ps[:, :, 2], ALU.mult))
                mk(V.tensor_reduce(tix[:, 1, :], ps[:, :, 0:2], AX_X, ALU.add))
                dve.wait_ge(s, c)
                mk(V.tensor_reduce(slot_gate[:, 0, :], ps[:, :, 3:6], AX_X, ALU.add))
                mk(V.tensor_tensor(tix[:, 2, :], tix[:, 1, :], tix[:, 0, :], ALU.subtract))
                dve.wait_ge(s, c)
                mk(V.tensor_tensor(tix[:, 3, :], tix[:, 2, :], slotbase, ALU.add))
                dve.wait_ge(s, c)
                mk(V.tensor_scalar(tix[:, 0, :], tix[:, 3, :], 4.0, jcol[:, 0:1], ALU.mult, ALU.add))
                dve.wait_ge(s, c)
                mk(V.tensor_copy(iv[:, 0, :], tix[:, 0, :]))
                dve.wait_ge(s, c)
                dve.sem_inc(idx_ready, 1)

            own.mark(V.memset(idx[:, :], 0))
            own.mark(V.memset(slot_gate, 0.0))
            own.settle()
            hot(0)
            dve.wait_ge(hot_ready, T)
            lower(0)
            dve.wait_ge(idx_done, 1)
            numbers(own.n)
            own.n += STEPS_IDX
            hot(1)
            dve.wait_ge(hot_ready, 2 * T + 1)
            lower(1)
            dve.wait_ge(idx_done, 2)
            dve.wait_ge(gathered, 48)
            numbers(own.n)
            own.n += STEPS_IDX
            hot(2)
            dve.wait_ge(hot_ready, 3 * T + 2)
            lower(2)
            for t in range(T):
                dve.wait_ge(bd_done, t + 1)
                own.mark(V.tensor_tensor(x2[:, t, 0:HALF], bank[3][:, :], x2[:, t, 0:HALF], ALU.add))
                own.mark(V.tensor_tensor(x2[:, t, HALF:D], bank[4][:, :], x2[:, t, HALF:D], ALU.add))
                own.settle()
                dve.sem_inc(acc_ready, 1)
            m = visits_less_two(dve)
            dve.wait_ge(idx_done, 3)
            dve.wait_ge(gathered, 96)
            numbers(own.n)
            own.n += STEPS_IDX
            hot(3)
            dve.wait_ge(hot_ready, 4 * T + 3)
            lower(3)

            def act_part(e, visit, base):
                s = own.s
                c = base
                dve.wait_ge(ht_done, visit)

                def bias(half):
                    v = bgu[:, half * KC:(half + 1) * KC, bass.ds(e, 1)]
                    return v.rearrange("p (j hh) o -> p hh j (o)", hh=2).to_broadcast([P, 2, 4, GROUP])

                def four(v):
                    return v.rearrange("p hh (j s) -> p hh j s", j=4)

                gsrc = [view(bank[5], 0, 2, P), view(bank[5], 256, 2, P), view(bank[6], 0, 2, P)]
                usrc = [view(bank[6], 256, 2, P), view(bank[7], 0, 2, P), view(bank[7], 256, 2, P)]
                for g in range(GROUPS):
                    V.tensor_tensor(four(g2[:, g, :, :]), four(gsrc[g]), bias(0), ALU.add).then_inc(s, 1)
                c = c + GROUPS
                dve.wait_ge(s, c)
                V.tensor_scalar(g2, g2, LIMIT, None, ALU.min).then_inc(g2_ready, 1)
                for g in range(GROUPS):
                    V.tensor_tensor(four(u2[:, g, :, :]), four(usrc[g]), bias(1), ALU.add).then_inc(s, 1)
                c = c + GROUPS
                dve.wait_ge(s, c)
                V.tensor_scalar(u2, u2, LIMIT, -LIMIT, ALU.min, ALU.max).then_inc(s, 1)
                c = c + 1
                dve.wait_ge(sg_ready, visit)
                V.tensor_tensor(g2, g2, sg, ALU.mult).then_inc(s, 1)
                c = c + 1
                dve.wait_ge(s, c)
                dve.wait_ge(d_used, visit * 4)
                flat = lambda v: v.rearrange("p g hh n -> p (g hh n)")
                V.scalar_tensor_tensor(out=flat(actT), in0=flat(u2), scalar=1.0, in1=flat(g2), op0=ALU.add,
                                       op1=ALU.mult).then_inc(act_ready, 1)

            LOOP_OWN = STEPS_IDX + 8
            with dve.Fori(1, m + 2) as i:
                base = (i - 1) * LOOP_OWN + own.n
                act_part((i - 1) % E, i, base)
                dve.wait_ge(idx_done, i + 3)
                dve.wait_ge(gathered, i * 48 + 96)
                dve.wait_ge(landed, i)
                dve.wait_ge(y_ready, i)
                numbers(base + 8)
                e3 = (i + 3) % E
                hot(e3)
                dve.wait_ge(hot_ready, (i + 4) * (T + 1) - 1)
                lower(e3)
            act_part(E - 1, m + 2, m * LOOP_OWN + (LOOP_OWN + own.n))
            dve.wait_ge(fss_ready, T + 2)
            dve.wait_ge(late_in, 32)
            for t in range(T):
                V.scalar_tensor_tensor(out=fin[:, t, :], in0=fin[:, t, :], scalar=rstdx[:, t:t + 1], in1=finw,
                                       op0=ALU.mult, op1=ALU.mult).then_inc(fin_ready, 1)

        @block.tensor
        def _(pe):
            M = nc.tensor.matmul
            TR = nc.tensor.transpose
            pe.wait_ge(consts_ready, 1)
            pe.wait_ge(param_in, 96)
            for j in range(CT):
                ins = TR(view(bank[3], 0, CT, 64)[:, j, 0:48], prow[0:48, j * P:(j + 1) * P], ident[0:48, 0:48])
            ins.then_inc(params_turned, 1)
            pe.wait_ge(bias_in, 16)
            for j in range(2 * KC):
                ins = TR(view(bank[4], 0, 2 * KC, E)[:, j, :], bgu_rows[:, j * P:(j + 1) * P], ident[0:E, 0:E])
            ins.then_inc(bias_turned, 1)
            for t in range(T):
                pe.wait_ge(xs_ready, t + 1)
                if t == 0:
                    pe.wait_ge(params_ready, 1)
                    pe.wait_ge(bias_ready, 1)
                for c in range(KC):
                    ins = TR(bank[c][:, t * P:(t + 1) * P], xr[:, t, c * P:(c + 1) * P], ident)
                    if t == T - 1:
                        ins.then_inc(x_turned, 1)
            pe.wait_ge(h_act, KC // 2)
            pe.wait_ge(h_dve, KC // 2)
            pe.wait_ge(gate_in, 48)
            for c in range(KC):
                ins = M(bank[3][0:2 * H, :], wab[:, c, :], hT[:, c, :], start=(c == 0), stop=(c == KC - 1))
            ins.then_inc(ab_done, 1)

            def gates(k):
                if k == 0:
                    pe.wait_ge(ab_copied, 1)
                    for t in range(T):
                        ins = TR(view(bank[4], 0, T, 2 * H)[:, t, :], ab_sb[:, t * P:(t + 1) * P],
                                 ident[0:2 * H, 0:2 * H])
                    ins.then_inc(ab_turned, 1)
                else:
                    pe.wait_ge(g_ready, 1)
                    pe.wait_ge(masks_ready, 1)
                    g = gg.rearrange("p t h -> p (t h)")
                    M(bank[4][:, 64:64 + TH], triu, g, start=True, stop=True)
                    M(bank[4][:, 96:96 + TH], blk, g, start=True, stop=True)
                    M(bank[4][:, 128:128 + TH], half0, g, start=True, stop=True)
                    M(bank[4][:, 128 + TH:128 + 2 * TH], half1, g, start=True, stop=True
                      ).then_inc(gsum_done, 1)

            def free_bank(s):
                p = s - 3
                if p < 0:
                    return
                kind, a, b = TILES[p]
                if kind == "cf":
                    pe.wait_ge(proj_dve, a + 1)
                elif kind == "qkv":
                    pe.wait_ge(proj_act, CT + 3 * a + b + 1)
                else:
                    pe.wait_ge(proj_dve, CT + a + 1)

            def proj(s, c):
                kind, a, b = TILES[s]
                if c == 0:
                    free_bank(s)
                if kind == "z":
                    u = NU - 2 + c // 4
                    pe.wait_ge(slot_in[u % 8], 32)
                    ins = M(bank_of(s)[:, :], hT[:, c, a * P:(a + 1) * P], unit_ap(u)[:, c % 4, :],
                            start=(c == 0), stop=(c == KC - 1))
                else:
                    u, half = UNIT_OF[s]
                    pe.wait_ge(slot_in[u % 8], 16 * (u // 8 + 1))
                    ins = M(bank_of(s)[:, :], unit_ap(u)[:, c, half * P:(half + 1) * P], hT[:, c, :],
                            start=(c == 0), stop=(c == KC - 1))
                if c == KC - 1:
                    ins.then_inc(proj_done, 1)

            def ssum(i):
                h, b = divmod(i, 3)
                if b == 2:
                    return
                pe.wait_ge(sq_ready, 2 * h + b + 1)
                if h >= 1:
                    pe.wait_ge(kv_ready, h)
                elif b == 1:
                    pe.wait_ge(ga_ready, 1)
                if h >= 2:
                    pe.wait_ge(uw_ready, 3 * (h - 1))
                M(bank[3 + b][:, :], ones, sq[b], start=True, stop=True).then_inc(ssum_done, 1)

            def gdn(h, k):
                q, kk = qT[h % 2], kT[h % 2]
                if k == 0:
                    if h >= 1:
                        pe.wait_ge(xx_ready, 11 * h)
                    for t in range(T):
                        ins = M(bank[7][:, t * P:(t + 1) * P], gg[:, t, h:h + 1].to_broadcast([P, P]), triu,
                                start=True, stop=True)
                    ins.then_inc(gcb_done, 1)
                if k == 1:
                    pe.wait_ge(norm_ready, 2 * h + 2)
                    for t in range(T):
                        c = slice(t * P, (t + 1) * P)
                        ins = M(bank[5][:, c], kk[:, c], kk[:, c], start=True, stop=True)
                    ins.then_inc(kk_done, 1)
                if k == 2:
                    for t in range(T):
                        c = slice(t * P, (t + 1) * P)
                        ins = M(bank[6][:, c], kk[:, c], q[:, c], start=True, stop=True)
                    ins.then_inc(qk_done, 1)
                if k == 3:
                    pe.wait_ge(silu_ready, 3 * h + 3)
                    pe.wait_ge(rs_ready, 2 * h + 2)
                    if h >= 1:
                        pe.wait_ge(uw_ready, 3 * h)
                    for t in range(T):
                        TR(bank[3][:, t * P:(t + 1) * P], kk[:, t * P:(t + 1) * P], ident)
                    for t in range(T):
                        ins = TR(bank[4][:, t * P:(t + 1) * P], vT[:, t * P:(t + 1) * P], ident)
                    ins.then_inc(kv_turned, 1)
                if k == 4:
                    pe.wait_ge(a_ready, h + 1)
                    for t in range(T):
                        ins = TR(bank[5][:, t * P:(t + 1) * P], Am[:, t, :], ident)
                    ins.then_inc(p_done, 1)
                if k == 5:
                    pe.wait_ge(in_ready, h + 1)
                    pe.wait_ge(egb_ready, h + 1)
                if 5 <= k < 15:
                    lv = 1 + (k - 5) // 2
                    s = LEVELS[lv]
                    if k % 2 == 1:
                        pe.wait_ge(xx_ready, 11 * h + 2 * lv)
                        for t in range(T):
                            ins = M(bank[5][:, t * P:(t + 1) * P], Am[:, t, :], XT[:, t, :], start=True, stop=True)
                        ins.then_inc(p_done, 1)
                    else:
                        pe.wait_ge(p_ready, 5 * h + lv)
                        if s < LEVELS[-1]:
                            for t in range(T):
                                M(bank[6][:, t * P:(t + 1) * P], Pm[:, t, :], X[:, t, :], start=True, stop=True)
                        for t in range(T):
                            ins = M(bank[7][:, t * P:(t + 1) * P], X[:, t, :], Pm[:, t, :], start=True,
                                    stop=True)
                        ins.then_inc(xx_done, 1)
                if k == 15:
                    pe.wait_ge(xx_ready, 11 * h + 11)
                    pe.wait_ge(kv_ready, h + 1)
                    pe.wait_ge(rs_ready, min(2 * (h + 1) + 2, 2 * H))
                    for t in range(T):
                        M(bank[3][:, t * P:(t + 1) * P], XT[:, t, :], uval[:, h, t, :], start=True, stop=True)
                    for t in range(T):
                        ins = M(bank[4][:, t * P:(t + 1) * P], kbgv[:, t, :], XT[:, t, :], start=True, stop=True)
                    ins.then_inc(uw_done, 1)

            AT = {5: (1, 3, 5, 7, 8), 6: (1, 2, 4, 5, 7, 8)}
            for s in range(NT):
                h, steps = gdn_of(s)
                at = AT.get(len(steps), ())
                for c in range(KC):
                    proj(s, c)
                    if s == 0 and c == 1:
                        gates(0)
                    if s == 2 and c == 1:
                        gates(1)
                    if c == 0 and s >= Q0 + 2:
                        if TILES[s - 2][0] == "qkv":
                            ssum(s - 2 - Q0)
                    for n, a in enumerate(at):
                        if a == c + 1:
                            gdn(h, steps[n])
            pe.wait_ge(cacc_ready, CT)
            pe.wait_ge(proj_dve, CT + T)
            for j in range(CT):
                ins = M(bank[1][:, :], ones, cacc[:, j, :], start=(j == 0), stop=(j == CT - 1))
            ins.then_inc(mean_done, 1)

            def ws(n):
                if n == 0:
                    pe.wait_ge(s_zero, 1)
                    pe.wait_ge(uw_ready, 3 * H)
                    pe.wait_ge(qd_ready, H)
                else:
                    pe.wait_ge(s_ready, H * n)
                if n >= 2:
                    pe.wait_ge(o_copied, n - 1)
                for h in range(H):
                    ins = M(bank[3 + n % 2][:, h * P:(h + 1) * P], wqT[:, h, n, :], S[:, h, :],
                            start=(h == 0), stop=False, skip_group_check=True)
                ins.then_inc(ws_done, 1)

            def su(n):
                t, f = divmod(n, 2)
                b = CHUNK * f
                ob = CHUNK - b
                pe.wait_ge(vn_ready, n + 1)
                for h in range(H):
                    ins = M(bank[5][:, h * P:(h + 1) * P], ktail[b:b + CHUNK, h, t, :], vn[b:b + CHUNK, h, :],
                            start=True, stop=True)
                ins.then_inc(su_done, 1)
                for h in range(H):
                    ins = M(bank[3 + n % 2][ob:ob + CHUNK, h * P:(h + 1) * P],
                            intraT[b:b + CHUNK, h, t, b:b + CHUNK], vn[b:b + CHUNK, h, :],
                            start=False, stop=True, skip_group_check=True)
                ins.then_inc(o_done, 1)

            def mix_turn(t):
                pe.wait_ge(mix_ready, t + 1)
                if t >= 1:
                    pe.wait_ge(mixT_ready, t)
                for h in range(H):
                    ins = TR(bank[6][:, h * P:(h + 1) * P], osb[t % 2][:, h, :], ident)
                ins.then_inc(mix_turned, 1)

            def outp(t, k0, k1):
                pair = PAIRS[t % 2]
                for k in range(k0, k1):
                    kc, half = divmod(k, 2)
                    c = (kc + H) % KC
                    if k == 0 and t >= 2:
                        pe.wait_ge(x2_ready, t - 1)
                    if k == 0 and t == 0:
                        pe.wait_ge(cmix_ready, CT)
                        pe.wait_ge(crs_ready, 1)
                        for i in range(4):
                            pe.wait_ge(slot_in[4 + i], 32)
                    if c == 0 and half == 0:
                        pe.wait_ge(mixT_ready, t + 1)
                    lhs = mixT[t % 2][:, c, :] if c < H else cacc[:, c - H, t * P:(t + 1) * P]
                    w = view(ring, (4 + c // 2) * SLOT, 2, D)[:, c % 2, half * HALF:(half + 1) * HALF]
                    ins = M(pair[half][:, :], lhs, w, start=(kc == 0), stop=(kc == KC - 1))
                if k1 == 16:
                    ins.then_inc(op_done, 1)

            def xn_turn(t):
                pe.wait_ge(xn_ready, t + 1)
                if t >= 1:
                    pe.wait_ge(xnT_ready, t)
                else:
                    pe.wait_ge(o_copied, 2 * T)
                for c in range(KC):
                    ins = TR(bank[3 + c // 4][:, (c % 4) * P:(c % 4 + 1) * P], xn[:, t % 2, c * P:(c + 1) * P],
                             ident)
                ins.then_inc(xn_turned, 1)

            def logits(t):
                pe.wait_ge(xnT_ready, t + 1)
                if t == 0:
                    pe.wait_ge(s_ready, H * 2 * T)
                    pe.wait_ge(wr_in, 48)
                else:
                    pe.wait_ge(lgT_copied, t)
                for r in range(2):
                    for j in range(4):
                        c = 4 * r + j
                        ins = M(bank[5][E * j:E * (j + 1), 0:P], router[:, c, :], xnT[t % 2][:, c, :],
                                start=(r == 0), stop=(r == 1), skip_group_check=True)
                ins.then_inc(lgT_done, 1)

            def logits_turn(t):
                pe.wait_ge(lgT_copied, t + 1)
                if t == 0:
                    pe.wait_ge(mixT_ready, T)
                else:
                    pe.wait_ge(mx_ready, t)
                TR(bank[6][:, 0:P], lgT, ident).then_inc(lg_done, 1)

            ws(0)
            su(0)
            pe.wait_ge(csq_ready, CT)
            for j in range(CT):
                ins = M(bank[0][:, :], ones, ubuf[:, j, 0:SEQ], start=(j == 0), stop=(j == CT - 1))
            ins.then_inc(var_done, 1)
            ws(1)
            su(1)
            ws(2)
            su(2)
            ws(3)
            mix_turn(0)
            su(3)
            outp(0, 0, 8)
            ws(4)
            outp(0, 8, 12)
            su(4)
            outp(0, 12, 16)
            ws(5)
            mix_turn(1)
            su(5)
            outp(1, 0, 8)
            ws(6)
            outp(1, 8, 12)
            su(6)
            outp(1, 12, 16)
            ws(7)
            mix_turn(2)
            su(7)
            outp(2, 0, 8)
            xn_turn(0)
            outp(2, 8, 16)
            mix_turn(3)
            logits(0)
            outp(3, 0, 4)
            logits_turn(0)
            outp(3, 4, 8)
            xn_turn(1)
            outp(3, 8, 12)
            logits(1)
            outp(3, 12, 16)
            logits_turn(1)
            for t in (2, 3):
                xn_turn(t)
                logits(t)
                logits_turn(t)
            pe.wait_ge(gate_ready, T)
            for t in range(T):
                for u in range(t + 1):
                    M(bank[6][:, t * E:(t + 1) * E], trif if u == t else ones, Msk[:, u, :], start=(u == 0),
                      stop=(u == t))
            for u in range(T):
                ins = M(bank[6][:, T * E:(T + 1) * E], ones, Msk[:, u, :], start=(u == 0), stop=(u == T - 1))
            ins.then_inc(pos_done, 1)

            ohv = view(onehot, 0, T, GROUPS, P)
            tgv = view(tg, 0, T, E, 6)

            def idx_mm(e, hot_wait):
                pe.wait_ge(hot_ready, hot_wait)
                for g in range(GROUPS):
                    for t in range(T):
                        ins = M(bank[7][:, 6 * g:6 * g + 6], ohv[:, t, g, :],
                                tgv[:, t, bass.ds(e, 1), :].rearrange("p o c -> p (o c)"),
                                start=(t == 0), stop=(t == T - 1))
                ins.then_inc(idx_done, 1)

            def xt_turn(g_wait):
                pe.wait_ge(gathered, g_wait)
                for g in range(GROUPS):
                    for hh in range(2):
                        b = bank[5] if g < 2 else bank[6]
                        c = (g % 2) * 256 + hh * P
                        ins = TR(b[:, c:c + P], xg[:, g, hh * P:(hh + 1) * P], ident)
                ins.then_inc(xt_done, 1)

            pe.wait_ge(route_ready, 1)
            idx_mm(0, T)
            xt_turn(48)
            pe.wait_ge(idx_ready, 1)
            idx_mm(1, 2 * T + 1)
            pe.wait_ge(bias_in, 32)
            for t in range(T):
                if t >= 1:
                    pe.wait_ge(gt_copied, t)
                TR(bank[2][0:E, 0:P], Gm[:, t, :], ident).then_inc(gt_done, 1)
                pe.wait_ge(gt_copied, t + 1)
                if t >= 1:
                    pe.wait_ge(acc_ready, t)
                for half in range(2):
                    ins = M(bank[3 + half][:, :], GT, bdn[:, half * HALF:(half + 1) * HALF], start=True,
                            stop=True)
                ins.then_inc(bd_done, 1)
            pe.wait_ge(acc_ready, T)
            pe.wait_ge(idx_ready, 2)
            idx_mm(2, 3 * T + 2)
            m = visits_less_two(pe)
            pe.sem_inc(d_used, 4)

            def gate_up(i):
                for c in range(KC):
                    pe.wait_ge(slot_in[c], i * 16 + 48)
                    w = view(ring, c * SLOT, 2, D)
                    for g in range(GROUPS):
                        for j in range(4):
                            ins = M(bank[g][GROUP * j:GROUP * (j + 1), :],
                                    xT[:, g, c % 2, (c // 2) * GROUP:(c // 2 + 1) * GROUP],
                                    w[:, :, j * QD:(j + 1) * QD], start=(c == 0), stop=(c == KC - 1))
                    ins.then_inc(gu_used, 1)

            def down(i):
                for u in range(4):
                    pe.wait_ge(slot_in[8 + u], i * 16 + 16)
                    w = view(dslots, u * SLOT, 2, D)
                    for cc in range(2):
                        c = 2 * u + cc
                        for g in range(GROUPS):
                            for j in range(4):
                                b, col = (bank[3], g * QD) if g < 2 else (bank[4], 0)
                                ins = M(b[GROUP * j:GROUP * (j + 1), col:col + QD],
                                        actT[:, g, c % 2, (c // 2) * GROUP:(c // 2 + 1) * GROUP],
                                        w[:, cc, j * QD:(j + 1) * QD],
                                        start=(c == 0 and g != 1), stop=(c == KC - 1), skip_group_check=True)
                    ins.then_inc(d_used, 1)

            def hid_turn(i):
                pe.wait_ge(hid_ready, (i + 1) * GROUPS)
                k = 0
                for half in range(2):
                    for g in range(GROUPS):
                        for hh in range(2):
                            b = bank[5 + k // 4]
                            ins = TR(b[:, (k % 4) * P:(k % 4 + 1) * P],
                                     hid[:, g, half * QD + hh * P:half * QD + (hh + 1) * P], ident)
                            k += 1
                ins.then_inc(ht_done, 1)

            pe.wait_ge(xt_ready, 1)
            gate_up(0)
            xt_turn(96)
            pe.wait_ge(xt_ready, 3)
            pe.wait_ge(idx_ready, 3)
            hid_turn(0)
            with pe.Fori(1, m + 2) as i:
                pe.wait_ge(hid_ready, i * GROUPS)
                gate_up(i)
                pe.wait_ge(act_ready, i)
                idx_mm((i + 2) % E, (i + 3) * (T + 1) - 1)
                xt_turn(i * 48 + 96)
                pe.wait_ge(y_ready, i)
                down(i - 1)
                pe.wait_ge(xt_ready, i * 2 + 3)
                pe.wait_ge(idx_ready, i + 3)
                hid_turn(i)
            pe.wait_ge(act_ready, m + 2)
            pe.wait_ge(y_ready, m + 2)
            down(m + 1)



_INS = ['x', 'attn_norm_w', 'w_in', 'gdn_conv_w', 'gdn_a_log', 'gdn_dt_bias', 'gdn_norm_w', 'cf_dw_w', 'cf_dw_b',
        'cf_ln_w', 'cf_ln_b', 'w_out', 'ffn_norm_w', 'w_router', 'b_router', 'w_gate_up', 'b_gate_up', 'w_down',
        'b_down', 'final_norm_w']


def kernel(**inputs):
    import numpy as _np
    import concourse.bacc as _bacc
    from concourse import mybir as _mybir
    from concourse.bass_utils import run_bass_kernel_spmd as _run

    nc = _bacc.Bacc("TRN2", target_bir_lowering=False, num_devices=1)
    arrays, args = {}, []
    for name in _INS:
        a = _np.ascontiguousarray(inputs[name])
        arrays[f"in_{name}_dram"] = a
        args.append(nc.dram_tensor(f"in_{name}_dram", a.shape, _mybir.dt.from_np(a.dtype), kind="ExternalInput").ap())
    shape = tuple(inputs['x'].shape)
    args.append(nc.dram_tensor("out_0_dram", shape, _mybir.dt.float32, kind="ExternalOutput").ap())
    block_kernel(nc, *args)
    r = _run(nc, [arrays], core_ids=[0])
    return r.results[0]["out_0_dram"]
```

```python
from contextlib import ExitStack

import concourse.bass as bass
from concourse import mybir

F32 = mybir.dt.float32
I32 = mybir.dt.int32
BF16 = mybir.dt.bfloat16
ALU = mybir.AluOpType
ACT = mybir.ActivationFunctionType
AX_X = mybir.AxisListType.X

P = 128
CHUNK = 64
TOP_K = 4
EPS = 1e-6
LIMIT = 7.0
ALPHA = 1.702
GROUP = 32
GROUPS = 4
CAP = GROUP * GROUPS
STAGES = 4


def block_kernel(nc, x, attn_norm_w, w_in, gdn_conv_w, gdn_a_log, gdn_dt_bias, gdn_norm_w, cf_dw_w, cf_dw_b,
                 cf_ln_w, cf_ln_b, w_out, ffn_norm_w, w_router, b_router, w_gate_up, b_gate_up, w_down,
                 b_down, final_norm_w, out):
    _, SEQ, D = x.shape
    H = gdn_a_log.shape[1]
    DK = gdn_norm_w.shape[1]
    QK = H * DK
    CF = cf_dw_w.shape[2]
    TAPS = cf_dw_w.shape[1]
    CONV = gdn_conv_w.shape[1]
    E = w_router.shape[2]
    T = SEQ // P
    KC = D // P
    CT = CF // P
    TH = T * H
    HALF = D // 2
    QD = D // 4
    PAD = TAPS - 1
    OFF_Z = 3 * QK
    OFF_BA = OFF_Z + QK
    OFF_CF = OFF_BA + 2 * H
    SLOT = 2 * D
    NR_ROWS = SEQ + P
    ROUNDS_MAX = -(-SEQ // CAP)
    assert DK == P and H == 4 and T == 4 and KC == 8 and CT == 4 and QK == 512

    x2d = x.rearrange("b s d -> (b s) d")
    out2d = out.rearrange("b s d -> (b s) d")
    win = w_in[0].rearrange("(c p) n -> p c n", p=P)
    wout = w_out[0].rearrange("(c p) n -> p c n", p=P)

    with ExitStack() as ctx:
        def sb(name, cols, dt=F32):
            return ctx.enter_context(nc.sbuf_tensor(name, [P, cols], dt))

        def sem(name):
            return ctx.enter_context(nc.semaphore(name))

        ring = sb("ring", 8 * SLOT)
        dslots = sb("dslots", 4 * SLOT)
        rows = sb("rows", T * D)
        hbuf = sb("hbuf", T * D)
        wq = sb("wq", 8 * 512)
        qkbuf = sb("qkbuf", 2 * 2 * SEQ)
        vbuf = sb("vbuf", SEQ)
        intra = sb("intra", H * SEQ)
        zrows = sb("zrows", T * QK)
        convbuf = sb("convbuf", 2 * (SEQ + CONV - 1) + 2 * SEQ)
        sqbuf = sb("sqbuf", 2 * SEQ)
        kbg = sb("kbg", SEQ)
        ffnw = sb("ffnw", D)
        consts = sb("consts", 17 * P)
        small = sb("small", 2048)
        slot_no = sb("slot_no", GROUPS * P, BF16)
        idx = sb("idx", STAGES * GROUPS, I32)
        n_iter = sb("n_iter", 1, I32)
        left = sb("left", ROUNDS_MAX * E + 2, I32)
        spare = sb("spare", 4 * H)
        count16 = sb("count16", 2 * P, BF16)
        tri16, ones16 = count16[:, 0:P], count16[:, P:2 * P]

        def view(t, start, *dims):
            n = 1
            for d in dims:
                n *= d
            v = t[:, start:start + n]
            names = "abcd"[:len(dims)]
            if len(dims) > 1:
                v = v.rearrange(f"p ({' '.join(names)}) -> p {' '.join(names)}",
                                **{names[i]: dims[i] for i in range(1, len(dims))})
            return v

        xr = view(rows, 0, T, D)
        ktail = view(rows, 0, H, T, P)
        uval = view(rows, H * SEQ, H, T, P)
        hT = view(hbuf, 0, KC, SEQ)
        x2 = view(hbuf, 0, T, D)
        wqT = view(wq, 0, H, 2 * T, P)
        bgu_rows = wq[0:E, 0:2 * D]
        ubuf = view(dslots, 0, CT, SEQ + PAD)
        o0 = CT * (SEQ + PAD)
        cacc = view(dslots, o0, CT, SEQ)
        o0 += CT * SEQ
        Am, X, XT, Pm, DT, Dm = (view(dslots, o0 + i * SEQ, T, P) for i in range(6))
        o0 += 6 * SEQ
        assert o0 <= 4 * SLOT
        xn = view(convbuf, 0, 2, D)
        zero_rows = intra[:, 0:D]
        thbuf = convbuf[:, 2 * (SEQ + CONV - 1):]
        o0 = 2 * D
        onehot = rows[:, o0:o0 + T * GROUPS * P // 2].bitcast(BF16)
        o0 += T * GROUPS * P // 2
        tg = rows[:, o0:o0 + T * E * 3].bitcast(BF16)
        qT = [qkbuf[:, 2 * SEQ * i:2 * SEQ * i + SEQ] for i in range(2)]
        kT = [qkbuf[:, 2 * SEQ * i + SEQ:2 * SEQ * (i + 1)] for i in range(2)]
        xnT = [view(qkbuf, D * i, KC, P) for i in range(2)]
        vT = vbuf[:, :]
        intraT = view(intra, 0, H, T, P)
        zr = view(zrows, 0, T, QK)
        kbgv = view(kbg, 0, T, P)
        preb = [convbuf[:, i * (SEQ + CONV - 1):(i + 1) * (SEQ + CONV - 1)] for i in range(2)]
        th = [thbuf[:, i * SEQ:(i + 1) * SEQ] for i in range(2)]
        sq = [sqbuf[:, i * SEQ:(i + 1) * SEQ] for i in range(2)]

        (ident, ones, triu, blk, half0, half1, strict, trif) = (consts[:, i * P:(i + 1) * P] for i in range(8))
        LEVELS = [1, 2, 4, 8, 16, 32]
        lmask = {s: consts[:, (8 + i) * P:(9 + i) * P] for i, s in enumerate(LEVELS)}
        lmask1t = consts[:, 16 * P:17 * P]
        epst = consts[:, 14 * P:14 * P + 1]
        zero1 = consts[:, 14 * P + 1:14 * P + 2]
        one1 = consts[:, 14 * P + 2:14 * P + 3]
        iota_e = consts[:, 14 * P + 32:14 * P + 64]
        thr = consts[:, 14 * P + 64:14 * P + 64 + ROUNDS_MAX - 1]
        slotbase = consts[:, 15 * P:15 * P + GROUPS]
        jcol = consts[:, 15 * P + 4:15 * P + 5]
        tokp = consts[:, 15 * P + 5:15 * P + 6]

        off = [0]

        def take(*dims):
            n = 1
            for d in dims:
                n *= d
            v = view(small, off[0], *dims)
            off[0] += n
            return v

        PT = take(CT, 52)
        bgu = take(2 * KC, E)
        wab = take(KC, 2 * H)
        ssx, rstdx = take(T), take(T)
        dtb, nA, bro = take(H), take(H), take(E)
        thb, beta, betah, ya, ym, ye, yl, gg = (take(T, H) for _ in range(8))
        gc, eg, ge, kts = (take(T, H) for _ in range(4))
        gtB = take(2, TH)
        rso, rsl = take(H), take(H)
        ss2, rstd2 = take(T), take(T)
        lg = take(E)
        m8, e4, pr4, sums = take(8), take(TOP_K), take(TOP_K), take(2)
        pos = take(T, E)
        slot_gate = take(STAGES, GROUPS)
        tix = take(4, GROUPS)
        rnd = take(8)
        leftf, cnt = take(E), take(E)
        assert off[0] <= 1600, off[0]
        Gm = view(kbg, 0, T, E)
        Msk = kbg[:, T * E:T * E + T * E // 2].bitcast(BF16).rearrange("p (t e) -> p t e", t=T)
        i8 = kbg[:, 2 * T * E:2 * T * E + 8]

        S = view(sqbuf, 0, H, P)
        vn = view(sqbuf, SEQ, H, P)
        osb = [view(dslots, CT * (SEQ + PAD) + CT * SEQ + i * SEQ, H, P) for i in range(2)]
        osq = view(dslots, CT * (SEQ + PAD) + CT * SEQ + 2 * SEQ, H, P)
        mixT = [view(dslots, CT * (SEQ + PAD) + CT * SEQ + (3 + i) * SEQ, H, P) for i in range(2)]
        normrow = view(dslots, CT * (SEQ + PAD) + CT * SEQ + 5 * SEQ, P)
        router = take(KC, E)
        assert off[0] <= 2048, off[0]
        lgT = vbuf[:, 0:P]
        GT = vbuf[0:E, :]
        bdn = intra[0:E, 0:D]
        ab_sb = thbuf[0:2 * H, 0:SEQ]
        prow = qkbuf[0:52, 0:CF]

        xg = view(wq, 0, GROUPS, QD)
        xT = view(wq, CAP * 8, GROUPS, 2, P)
        hid = view(wq, CAP * 16, GROUPS, 512)
        sg = view(zrows, 0, GROUPS, 2, P)
        u2 = view(zrows, CAP * 8, GROUPS, 2, P)
        g2 = view(intra, 0, GROUPS, 2, P)
        actT = view(intra, CAP * 8, GROUPS, 2, P)
        yb = view(rows, 0, GROUPS, QD)
        finw = rows[:, D:2 * D]
        fin = view(hbuf, 0, T, D)

        bank = [ctx.enter_context(nc.psum_tensor(f"bank{i}", [P, 512], F32)) for i in range(8)]

        xn_dram = nc.dram_tensor("xn_rows", [NR_ROWS, D], F32, kind="Internal").ap()
        acc_dram = nc.dram_tensor("acc_rows", [NR_ROWS, D], F32, kind="Internal").ap()
        xn_q = xn_dram.rearrange("r (j n) -> (r j) n", j=4)
        acc_q = acc_dram.rearrange("r (j n) -> (r j) n", j=4)

        x_in = [sem(f"x_in{t}") for t in range(T)]
        xres_in = [sem(f"xres_in{t}") for t in range(T)]
        slot_in = [sem(f"slot_in{i}") for i in range(12)]
        param_in, gate_in, bias_in, late_in, wr_in = (sem(n) for n in
                                                      ("param_in", "gate_in", "bias_in", "late_in", "wr_in"))
        fin_in = [sem(f"fin_in{t}") for t in range(T)]
        zero_out, acc_out, last_out = sem("zero_out"), sem("acc_out"), sem("last_out")
        xn_out = [sem(f"xn_out{i}") for i in range(2)]
        act_self, dve_self, pool_self = sem("act_self"), sem("dve_self"), sem("pool_self")
        consts_ready, masks_ready, zeros_ready = sem("consts_ready"), sem("masks_ready"), sem("zeros_ready")
        params_turned, params_ready, bias_turned, bias_ready = (sem(n) for n in (
            "params_turned", "params_ready", "bias_turned", "bias_ready"))
        rstdx_ready, xs_ready, x_turned, h_act, h_dve = (sem(n) for n in (
            "rstdx_ready", "xs_ready", "x_turned", "h_act", "h_dve"))
        ab_done, ab_copied, ab_turned, g_ready, gsum_done, gc_ready = (sem(n) for n in (
            "ab_done", "ab_copied", "ab_turned", "g_ready", "gsum_done", "gc_ready"))
        ab_dve, ab_act, ga_ready = sem("ab_dve"), sem("ab_act"), sem("ga_ready")
        proj_done, proj_act, proj_dve = (sem(n) for n in ("proj_done", "proj_act", "proj_dve"))
        conv_ready, tanh_ready, silu_ready, sq_ready = (sem(n) for n in (
            "conv_ready", "tanh_ready", "silu_ready", "sq_ready"))
        ssum_done, rs_ready, norm_ready = sem("ssum_done"), sem("rs_ready"), sem("norm_ready")
        gcb_done, kk_done, qk_done, kv_turned = (sem(n) for n in ("gcb_done", "kk_done", "qk_done", "kv_turned"))
        diff_ready, dec_ready, dmask_ready, egb_ready = (sem(n) for n in (
            "diff_ready", "dec_ready", "dmask_ready", "egb_ready"))
        a_ready, in_ready, kv_ready, qd_ready = (sem(n) for n in ("a_ready", "in_ready", "kv_ready", "qd_ready"))
        p_done, p_ready, xx_done, xx_ready = (sem(n) for n in ("p_done", "p_ready", "xx_done", "xx_ready"))
        uw_done, uw_ready = sem("uw_done"), sem("uw_ready")
        cacc_ready, mean_done, xc_ready, csq_ready, var_done, crs_ready, cy_ready, cth_ready, cmix_ready = (
            sem(n) for n in ("cacc_ready", "mean_done", "xc_ready", "csq_ready", "var_done", "crs_ready",
                             "cy_ready", "cth_ready", "cmix_ready"))

        ws_done, vn_ready, su_done, s_ready, o_done, o_copied = (sem(n) for n in (
            "ws_done", "vn_ready", "su_done", "s_ready", "o_done", "o_copied"))
        osq_ready, oss_ready, ors_ready, mix_ready, mix_turned, mixT_ready = (sem(n) for n in (
            "osq_ready", "oss_ready", "ors_ready", "mix_ready", "mix_turned", "mixT_ready"))

        op_done, x2_ready, rstd2_ready, xn_ready, xn_turned, xnT_ready = (sem(n) for n in (
            "op_done", "x2_ready", "rstd2_ready", "xn_ready", "xn_turned", "xnT_ready"))
        lgT_done, lgT_copied, lg_done, mx_ready, ex_ready, gate_ready = (sem(n) for n in (
            "lgT_done", "lgT_copied", "lg_done", "mx_ready", "ex_ready", "gate_ready"))
        pos_done, route_ready = sem("pos_done"), sem("route_ready")
        gt_done, gt_copied, bd_done, acc_ready = (sem(n) for n in ("gt_done", "gt_copied", "bd_done", "acc_ready"))
        hot_ready, idx_done, idx_ready, gathered, xt_done, xt_ready = (sem(n) for n in (
            "hot_ready", "idx_done", "idx_ready", "gathered", "xt_done", "xt_ready"))
        gu_used, hid_ready, ht_done, g2_ready, sg_ready, act_ready = (sem(n) for n in (
            "gu_used", "hid_ready", "ht_done", "g2_ready", "sg_ready", "act_ready"))
        d_used, y_ready, scattered = sem("d_used"), sem("y_ready"), sem("scattered")
        fss_ready, fin_ready, pool_step, landed = (sem(n) for n in ("fss_ready", "fin_ready", "pool_step",
                                                                    "landed"))
        half_read, router_ready = sem("half_read"), sem("router_ready")

        class Own:

            def __init__(self, eng, s):
                self.eng, self.s, self.n = eng, s, 0

            def mark(self, ins):
                ins.then_inc(self.s, 1)
                self.n += 1

            def settle(self):
                self.eng.wait_ge(self.s, self.n)

        TILES = [("cf", i // 2, i % 2) for i in range(2 * CT)]
        TILES += [("qkv", i // 3, i % 3) for i in range(3 * H)]
        TILES += [("z", t, 0) for t in range(T)]
        NT = len(TILES)
        Q0 = 2 * CT
        Z0 = Q0 + 3 * H
        CF_A, CF_B = OFF_CF, OFF_CF + CF
        UNITS = [CF_A, CF_B, CF_A + 256, CF_B + 256, 0, QK, 2 * QK, 256, QK + 256, 2 * QK + 256]
        UNIT_OF = {}
        for i in range(2 * CT):
            UNIT_OF[i] = (2 * (i // 4) + i % 2, (i // 2) % 2)
        for i in range(3 * H):
            UNIT_OF[Q0 + i] = (4 + 3 * (i // 6) + i % 3, (i // 3) % 2)
        NU = len(UNITS) + 2
        LAST_TILE = {}
        for i, (u, _) in UNIT_OF.items():
            LAST_TILE[u] = max(LAST_TILE.get(u, 0), i)
        LAST_TILE[NU - 2] = LAST_TILE[NU - 1] = NT - 1
        GDN_STEPS = 16
        PER_SLOT = [5, 5, 6]

        def gdn_of(s):
            if s < Q0 + 4 or s >= Q0 + 4 + 3 * H:
                return None, []
            h, k = divmod(s - Q0 - 4, 3)
            a = sum(PER_SLOT[:k])
            return h, list(range(a, a + PER_SLOT[k]))

        def unit_ap(u):
            return view(ring, (u % 8) * SLOT, KC, 256) if u < NU - 2 else view(ring, (u % 8) * SLOT, 4, 512)

        def tokens_left(engine, i):
            return engine.value_load(left[0:1, bass.ds(i, 1)], min_val=0, max_val=SEQ)

        def visits_less_two(engine):
            return engine.value_load(n_iter[0:1, 0:1], min_val=E - 2, max_val=E * ROUNDS_MAX - 2)

        def bank_of(s):
            return bank[s % 3]

        PAIRS = [(bank[0], bank[1]), (bank[2], bank[7])]

        block = ctx.enter_context(nc.Block())

        @block.sync
        def _(sp):
            sp.dma_start(xr[:, 0, :], x2d[0:P, :]).then_inc(x_in[0], 16)
            for i, v in enumerate((cf_dw_b, cf_ln_w, cf_ln_b)):
                sp.dma_start(prow[TAPS + i:TAPS + i + 1, :], v).then_inc(param_in, 16)
            sp.dma_start(prow[34:46, :], gdn_conv_w[0].rearrange("w (s c) -> (w s) c", s=3)).then_inc(param_in, 16)
            sp.dma_start(prow[46:48, :], attn_norm_w.rearrange("o (r c) -> (o r) c", r=2)).then_inc(param_in, 16)
            sp.dma_start(prow[48:50, :], ffn_norm_w.rearrange("o (r c) -> (o r) c", r=2)).then_inc(param_in, 16)
            for t in range(1, T):
                sp.dma_start(xr[:, t, :], x2d[t * P:(t + 1) * P, :]).then_inc(x_in[t], 16)
            for u in range(NU):
                if u >= 8:
                    sp.wait_ge(proj_done, LAST_TILE[u - 8] + 1)
                if u < NU - 2:
                    src = win[:, :, UNITS[u]:UNITS[u] + 256]
                else:
                    c = 4 * (u - NU + 2)
                    src = win[:, c:c + 4, OFF_Z:OFF_Z + QK]
                sp.dma_start(unit_ap(u), src).then_inc(slot_in[u % 8], 16)
            for i in range(4):
                sp.wait_ge(proj_done, LAST_TILE[4 + i] + 1)
                sp.dma_start(view(ring, (4 + i) * SLOT, 2, D), wout[:, 2 * i:2 * i + 2, :]).then_inc(
                    slot_in[4 + i], 16)

            def gate_up(i, c):
                e = i % E
                sp.dma_start(view(ring, c * SLOT, SLOT), w_gate_up[0, e, c * P:(c + 1) * P, :]).then_inc(
                    slot_in[c], 16)

            def down(i, u):
                e = i % E
                sp.dma_start(view(dslots, u * SLOT, 2, D),
                             w_down[0, e, 2 * u * P:(2 * u + 2) * P, :].rearrange("(c p) n -> p c n", p=P)
                             ).then_inc(slot_in[8 + u], 16)

            sp.wait_ge(proj_done, NT)
            for t in range(T):
                sp.dma_start(x2[:, t, :], x2d[t * P:(t + 1) * P, :]).then_inc(xres_in[t], 16)
            for c in range(KC):
                if c == 4:
                    sp.wait_ge(op_done, T)
                if c == 6:
                    sp.wait_ge(xn_ready, T)
                gate_up(0, c)
            for u in range(4):
                if u == 2:
                    sp.wait_ge(gathered, 16 * GROUPS)
                down(0, u)
            sp.wait_ge(route_ready, 1)
            m = visits_less_two(sp)
            for c in range(KC):
                sp.wait_ge(gu_used, c + 1)
                gate_up(1, c)
            with sp.Fori(2, m + 2) as i:
                for c in range(KC):
                    sp.wait_ge(gu_used, (i - 1) * KC + c + 1)
                    gate_up(i, c)
                for u in range(4):
                    sp.wait_ge(d_used, (i - 1) * 4 + u + 1)
                    down(i - 1, u)
            for u in range(4):
                sp.wait_ge(gu_used, m * KC + (KC + 2 * u + 2))
                sp.dma_start(view(ring, u * SLOT, 2, D),
                             w_down[0, E - 1, 2 * u * P:(2 * u + 2) * P, :].rearrange("(c p) n -> p c n", p=P)
                             ).then_inc(slot_in[u], 16)
            sp.wait_ge(scattered, m * (16 * GROUPS) + 32 * GROUPS)
            sp.wait_ge(acc_out, 16 * T)
            for t in range(T):
                sp.dma_start(fin[:, t, :], acc_dram[t * P:(t + 1) * P, :]).then_inc(fin_in[t], 16)
            for t in range(T):
                sp.wait_ge(fin_ready, t + 1)
                sp.dma_start(out2d[t * P:(t + 1) * P, :], fin[:, t, :]).then_inc(last_out, 16)
            sp.wait_ge(last_out, 16 * T)

        @block.gpsimd
        def _(pool):
            own = Own(pool, pool_self)

            def sel(v, pattern, base, ch, op=ALU.is_ge):
                own.mark(nc.gpsimd.affine_select(out=v, in_=v, compare_op=op, fill=0.0, base=base,
                                                 pattern=pattern, channel_multiplier=ch))
                own.settle()

            own.mark(nc.gpsimd.memset(consts[:, 0:14 * P], 1.0))
            own.mark(nc.gpsimd.memset(lmask1t, 1.0))
            for b in preb:
                own.mark(nc.gpsimd.memset(b[:, 0:CONV - 1], 0.0))
            own.mark(nc.gpsimd.memset(epst, EPS))
            own.mark(nc.gpsimd.memset(zero1, 0.0))
            own.mark(nc.gpsimd.memset(one1, 1.0))
            own.settle()
            nc.gpsimd.affine_select(out=ident, in_=ident, compare_op=ALU.is_equal, fill=0.0, base=0,
                                    pattern=[[-1, P]], channel_multiplier=1).then_inc(consts_ready, 1)
            nc.gpsimd.memset(zero_rows, 0.0).then_inc(zeros_ready, 1)
            pool.wait_ge(zeros_ready, 1)
            pool.dma_start(xn_dram[SEQ:NR_ROWS, :], zero_rows).then_inc(zero_out, 16)
            pool.dma_start(acc_dram[SEQ:NR_ROWS, :], zero_rows).then_inc(zero_out, 16)
            two = lambda v: v.rearrange("p (i w) -> p i w", i=2)
            sel(triu, [[1, P]], 0, -1)
            sel(two(triu), [[-CHUNK, 2], [0, CHUNK]], 0, 1)
            sel(two(blk), [[-CHUNK, 2], [0, CHUNK]], 0, 1)
            sel(two(blk), [[CHUNK, 2], [0, CHUNK]], CHUNK - 1, -1)
            sel(half0, [[0, P]], CHUNK - 1, -1)
            sel(half1, [[0, P]], -CHUNK, 1)
            sel(strict, [[-1, P]], -1, 1)
            sel(two(strict), [[CHUNK, 2], [0, CHUNK]], CHUNK - 1, -1)
            sel(trif, [[1, P]], 0, -1)
            for s in LEVELS:
                n = P // (2 * s)
                v = lmask[s].rearrange("p (i w) -> p i w", i=n)
                sel(v, [[-2 * s, n], [0, 2 * s]], 0, 1)
                sel(v, [[2 * s, n], [0, 2 * s]], s - 1, -1)
                sel(v, [[0, n], [1, 2 * s]], -s, 0)
            v = lmask1t.rearrange("p (i w) -> p i w", w=2)
            sel(v, [[2, P // 2], [0, 2]], 1, -1)
            sel(v, [[-2, P // 2], [0, 2]], -1, 1)
            sel(v, [[0, P // 2], [-1, 2]], 0, 0)
            own.mark(nc.gpsimd.iota(iota_e, pattern=[[1, E]], base=0, channel_multiplier=0,
                                    allow_small_or_imprecise_dtypes=True))
            own.mark(nc.gpsimd.iota(thr, pattern=[[CAP, ROUNDS_MAX - 1]], base=CAP, channel_multiplier=0,
                                    allow_small_or_imprecise_dtypes=True))
            own.mark(nc.gpsimd.iota(tokp, pattern=[[0, 1]], base=0, channel_multiplier=1,
                                    allow_small_or_imprecise_dtypes=True))
            own.mark(nc.gpsimd.iota(view(slot_no, 0, GROUPS, 4, GROUP),
                                    pattern=[[GROUP, GROUPS], [0, 4], [1, GROUP]], base=0, channel_multiplier=0,
                                    allow_small_or_imprecise_dtypes=True))
            for j in range(4):
                a = GROUP * j
                own.settle()
                own.mark(nc.gpsimd.iota(slotbase[a:a + GROUP, :], pattern=[[GROUP, GROUPS]], base=SEQ,
                                        channel_multiplier=1, allow_small_or_imprecise_dtypes=True))
                own.mark(nc.gpsimd.memset(jcol[a:a + GROUP, :], float(j)))
            own.settle()
            nc.gpsimd.memset(ubuf[:, :, 0:PAD], 0.0).then_inc(masks_ready, 1)

            def square(h, part):
                n = 2 * h + part
                pool.wait_ge(silu_ready, 3 * h + part + 1)
                if n >= 2:
                    pool.wait_ge(norm_ready, n - 1)
                src = (qT, kT)[part][h % 2]
                nc.gpsimd.tensor_tensor(sq[n % 2], src, src, ALU.mult).then_inc(sq_ready, 1)

            def mask_decays(h):
                bc = lambda m: m.rearrange("p (o c) -> p o c", o=1).to_broadcast([P, T, P])
                pool.wait_ge(dec_ready, 2 * h + 1)
                nc.gpsimd.tensor_tensor(Dm, Dm, bc(strict), ALU.mult).then_inc(dmask_ready, 1)
                pool.wait_ge(dec_ready, 2 * h + 2)
                nc.gpsimd.tensor_tensor(DT, DT, bc(triu), ALU.mult).then_inc(dmask_ready, 1)

            pool.wait_ge(ga_ready, 1)
            for s in range(Q0, NT + 1):
                h, steps = gdn_of(s)
                if 0 in steps:
                    mask_decays(h)
                i = s - 1 - Q0
                if 0 <= i < 3 * H and i % 3 < 2:
                    square(*divmod(i, 3))
            pool.wait_ge(xc_ready, CT)
            for j in range(CT):
                nc.gpsimd.tensor_tensor(ubuf[:, j, 0:SEQ], cacc[:, j, :], cacc[:, j, :], ALU.mult).then_inc(
                    csq_ready, 1)
            for t in range(T):
                pool.wait_ge(o_copied, 2 * t + 2)
                if t >= 1:
                    pool.wait_ge(oss_ready, t)
                nc.gpsimd.tensor_tensor(osq, osb[t % 2], osb[t % 2], ALU.mult).then_inc(osq_ready, 1)

            for t in range(T):
                pool.wait_ge(xn_ready, t + 1)
                pool.dma_start(xn_dram[t * P:(t + 1) * P, :], xn[:, t % 2, :]).then_inc(xn_out[t % 2], 16)
            for i in range(2):
                pool.wait_ge(xn_out[i], 16 * T // 2)
            pool.wait_ge(zero_out, 32)

            def gather(g):
                pool.indirect_dma_start(out=xg[:, g, :], out_offset=None, in_=xn_q,
                                        in_offset=bass.IndirectOffsetOnAxis(ap=idx[:, g:g + 1], axis=0),
                                        bounds_check=None).then_inc(gathered, 16)

            def scatter(g, stage):
                c = stage * GROUPS + g
                pool.indirect_dma_start(out=acc_q,
                                        out_offset=bass.IndirectOffsetOnAxis(ap=idx[:, c:c + 1], axis=0),
                                        in_=yb[:, g, :], in_offset=None,
                                        compute_op=ALU.add).then_inc(scattered, 16)

            def idle(k, done):
                pool.dma_start(spare[0:1, k * H:(k + 1) * H], gdn_dt_bias[0:1, :]).then_inc(done, 16)

            def full_or_idle(i, full, empty):
                tokens = tokens_left(pool, i)
                with pool.If(tokens > 2 * GROUP):
                    full(2)
                    with pool.If(tokens > 3 * GROUP):
                        full(3)
                    with pool.Else():
                        empty(3)
                with pool.Else():
                    empty(2)
                    empty(3)

            pool.wait_ge(idx_ready, 1)
            for g in range(GROUPS):
                gather(g)
            pool.wait_ge(idx_ready, 2)
            pool.wait_ge(xt_done, 1)
            for g in range(GROUPS):
                gather(g)
            for t in range(T):
                pool.wait_ge(acc_ready, t + 1)
                pool.dma_start(acc_dram[t * P:(t + 1) * P, :], x2[:, t, :]).then_inc(acc_out, 16)
            pool.wait_ge(acc_out, 16 * T)
            pool.wait_ge(route_ready, 1)
            m = visits_less_two(pool)
            pool.sem_inc(landed, 1)
            pool.wait_ge(idx_ready, 3)
            pool.wait_ge(xt_done, 2)
            for g in range(GROUPS):
                gather(g)
            with pool.Fori(1, m + 2) as i:
                pool.wait_ge(idx_ready, i + 3)
                pool.wait_ge(xt_done, i + 2)
                pool.sem_inc(pool_step, 1)
                for g in range(2):
                    gather(g)
                full_or_idle(i + 2, gather, lambda g: idle(g - 2, gathered))
                pool.wait_ge(y_ready, i + 1)
                pool.sem_inc(pool_step, 1)
                for g in range(2):
                    scatter(g, 3)
                full_or_idle(i - 1, lambda g: scatter(g, 3), lambda g: idle(g, scattered))
                pool.wait_ge(scattered, i * (16 * GROUPS))
                pool.sem_inc(landed, 1)
            pool.wait_ge(y_ready, m + 3)
            pool.sem_inc(pool_step, 1)
            for g in range(GROUPS):
                scatter(g, 2)
            pool.wait_ge(gathered, m * (16 * GROUPS) + 64 * GROUPS)
            pool.wait_ge(scattered, m * (16 * GROUPS) + 32 * GROUPS)

        @block.scalar
        def _(act):
            own = Own(act, act_self)
            A = nc.scalar.activation
            act.preload_act_table_set("natural_log_exp_and_others")
            act.dma_start(prow[0:TAPS, :], cf_dw_w[0]).then_inc(param_in, 16)
            act.dma_start(wab, win[:, :, OFF_BA:OFF_BA + 2 * H]).then_inc(gate_in, 16)
            act.dma_start(dtb, gdn_dt_bias[0:1, :].to_broadcast([P, H])).then_inc(gate_in, 16)
            act.dma_start(nA, gdn_a_log[0:1, :].to_broadcast([P, H])).then_inc(gate_in, 16)


            act.wait_ge(consts_ready, 1)
            for t in range(T):
                act.wait_ge(x_in[t], 16)
                own.mark(A(zrows[:, (t % 2) * D:(t % 2) * D + D], xr[:, t, :], ACT.Square,
                           accum_out=ssx[:, t:t + 1]))
                own.settle()
                own.mark(A(rstdx[:, t:t + 1], ssx[:, t:t + 1], ACT.Ln, bias=epst, scale=1.0 / D))
                own.settle()
                A(rstdx[:, t:t + 1], rstdx[:, t:t + 1], ACT.Exp, scale=-0.5).then_inc(rstdx_ready, 1)

            act.dma_start(bgu_rows, b_gate_up[0]).then_inc(bias_in, 16)
            act.dma_start(router, w_router[0].rearrange("(c p) e -> p c e", p=P)).then_inc(wr_in, 16)
            act.dma_start(bro, b_router[0:1, :].to_broadcast([P, E])).then_inc(wr_in, 16)
            act.dma_start(ffnw[:, :], ffn_norm_w[0:1, :].to_broadcast([P, D])).then_inc(wr_in, 16)
            act.wait_ge(params_ready, 1)
            for c in range(0, KC, 2):
                act.wait_ge(x_turned, c + 1)
                A(hT[:, c, :], bank[c][:, :], ACT.Copy, scale=PT[:, c % CT, 46 + c // CT:47 + c // CT]
                  ).then_inc(h_act, 1)
            act.wait_ge(ab_done, 1)
            A(ab_sb, bank[3][0:2 * H, :], ACT.Copy).then_inc(ab_copied, 1)

            act.wait_ge(ab_turned, 1)
            act.wait_ge(gate_in, 48)
            act.wait_ge(ab_dve, 1)
            A(thb, view(bank[4], 0, T, 2 * H)[:, :, 0:H], ACT.Tanh, scale=0.5).then_inc(ab_act, 1)
            act.preload_act_table_set("natural_log_exp_and_others")
            own.mark(A(nA, nA, ACT.Exp))
            own.mark(A(ye, ya, ACT.Exp, scale=-1.0))
            own.settle()
            A(yl, ye, ACT.Ln, bias=one1).then_inc(ab_act, 1)
            act.wait_ge(gsum_done, 1)
            act.wait_ge(gc_ready, 1)
            own.mark(A(eg, gc, ACT.Exp))
            own.mark(A(kts, kts, ACT.Exp))
            A(gtB, view(bank[4], 128, 2, TH), ACT.Exp).then_inc(ab_act, 1)

            def tile_copy(s):
                kind, a, b = TILES[s]
                if kind == "cf":
                    if b == 1:
                        act.wait_ge(proj_done, s + 1)
                        if a >= 2:
                            act.wait_ge(proj_dve, a - 1)
                        if a == 0:
                            act.wait_ge(ab_turned, 1)
                        A(th[a % 2], bank_of(s)[:, :], ACT.Tanh, scale=0.5).then_inc(proj_act, 1)
                elif kind == "qkv":
                    i = 3 * a + b
                    act.wait_ge(proj_done, s + 1)
                    if i >= 2:
                        act.wait_ge(conv_ready, i - 1)
                    A(preb[i % 2][:, CONV - 1:], bank_of(s)[:, :], ACT.Copy).then_inc(proj_act, 1)
                else:
                    act.wait_ge(proj_done, s + 1)
                    act.wait_ge(silu_ready, 3 * H)
                    if a >= 1:
                        act.wait_ge(proj_dve, CT + a)
                    A(th[1], bank_of(s)[:, :], ACT.Tanh, scale=0.5).then_inc(proj_act, 1)

            def tile_tanh(s):
                kind, a, b = TILES[s]
                if kind != "qkv":
                    return
                i = 3 * a + b
                act.wait_ge(conv_ready, i + 1)
                dst = (qT[a % 2], kT[a % 2], vT)[b]
                if i >= 1:
                    act.wait_ge(silu_ready, i)
                if i == 0:
                    act.wait_ge(proj_dve, CT)
                A(th[1], dst, ACT.Tanh, scale=0.5).then_inc(tanh_ready, 1)

            def tile_rs(s):
                kind, a, b = TILES[s]
                if kind != "qkv" or b == 2:
                    return
                n = 2 * a + b
                act.wait_ge(ssum_done, n + 1)
                v = sq[n % 2]
                own.mark(A(v, bank[3 + b][:, :], ACT.Ln, bias=epst, scale=0.25))
                own.settle()
                A(v, v, ACT.Exp, scale=-0.5).then_inc(rs_ready, 1)

            def gdn(h, k):
                if k == 0:
                    act.wait_ge(gcb_done, h + 1)
                    if h >= 1:
                        act.wait_ge(qd_ready, h)
                    act.wait_ge(diff_ready, 2 * h + 1)
                    A(Dm, Dm, ACT.Exp).then_inc(dec_ready, 1)
                    act.wait_ge(diff_ready, 2 * h + 2)
                    A(DT, DT, ACT.Exp).then_inc(dec_ready, 1)
                    A(th[0], bank[7][:, :], ACT.Exp).then_inc(egb_ready, 1)
                if k == GDN_STEPS - 1:
                    act.wait_ge(uw_done, h + 1)
                    A(uval[:, h, :, :], view(bank[3], 0, T, P), ACT.Copy).then_inc(uw_ready, 1)
                    w = view(bank[4], 0, T, 2, CHUNK)
                    d = wqT[:, h, :, :].rearrange("p (t f) c -> p t f c", f=2)
                    A(d[:, :, 0, 0:CHUNK], w[:, :, 0, :], ACT.Copy).then_inc(uw_ready, 1)
                    A(d[:, :, 1, CHUNK:P], w[:, :, 1, :], ACT.Copy).then_inc(uw_ready, 1)

            for s in range(NT + 1):
                h, steps = gdn_of(s)
                if 0 in steps:
                    gdn(h, 0)
                if s >= 1:
                    tile_copy(s - 1)
                    tile_tanh(s - 1)
                if s >= 2:
                    tile_rs(s - 2)
                if GDN_STEPS - 1 in steps:
                    gdn(h, GDN_STEPS - 1)
                if s == 5:
                    act.wait_ge(bias_turned, 1)
                    A(bgu.rearrange("p a b -> p (a b)"), bank[5][:, :], ACT.Copy).then_inc(bias_ready, 1)
            act.wait_ge(a_ready, H)
            act.dma_start(normrow, gdn_norm_w[0:1, :].to_broadcast([P, P])).then_inc(late_in, 16)
            act.preload_act_table_set("natural_log_exp_and_others")

            def conf_rstd():
                crs = vbuf[:, :]
                act.wait_ge(var_done, 1)
                act.wait_ge(kv_ready, H)
                own.mark(A(crs, bank[0][:, :], ACT.Ln, bias=epst, scale=1.0 / CF))
                own.settle()
                A(crs, crs, ACT.Exp, scale=-0.5).then_inc(crs_ready, 1)

            def o_copy(n):
                t, f = divmod(n, 2)
                ob, b = (CHUNK, 0) if f == 0 else (0, CHUNK)
                act.wait_ge(o_done, n + 1)
                if t >= 2:
                    act.wait_ge(mix_turned, t - 1)
                A(osb[t % 2][b:b + CHUNK, :, :], view(bank[3 + n % 2], 0, H, P)[ob:ob + CHUNK, :, :],
                  ACT.Copy).then_inc(o_copied, 1)

            def o_rstd(t):
                act.wait_ge(oss_ready, t + 1)
                if t >= 1:
                    act.wait_ge(mix_ready, t)
                own.mark(A(rsl, rso, ACT.Ln, bias=epst, scale=1.0 / DK))
                own.settle()
                A(rsl, rsl, ACT.Exp, scale=-0.5).then_inc(ors_ready, 1)

            def mixT_copy(t):
                act.wait_ge(mix_turned, t + 1)
                if t >= 2:
                    act.wait_ge(op_done, t - 1)
                A(mixT[t % 2], view(bank[6], 0, H, P), ACT.Copy).then_inc(mixT_ready, 1)

            def x2_rstd(t):
                act.wait_ge(x2_ready, t + 1)
                own.mark(A(zrows[:, 0:D], x2[:, t, :], ACT.Square, accum_out=ss2[:, t:t + 1]))
                own.settle()
                own.mark(A(rstd2[:, t:t + 1], ss2[:, t:t + 1], ACT.Ln, bias=epst, scale=1.0 / D))
                own.settle()
                A(rstd2[:, t:t + 1], rstd2[:, t:t + 1], ACT.Exp, scale=-0.5).then_inc(rstd2_ready, 1)

            def xnT_copy(t):
                act.wait_ge(xn_turned, t + 1)
                if t >= 2:
                    act.wait_ge(lgT_done, t - 1)
                A(xnT[t % 2][:, 0:4, :], view(bank[3], 0, 4, P), ACT.Copy)
                A(xnT[t % 2][:, 4:8, :], view(bank[4], 0, 4, P), ACT.Copy).then_inc(xnT_ready, 1)

            def lgT_copy(t):
                act.wait_ge(lgT_done, t + 1)
                if t >= 1:
                    act.wait_ge(lg_done, t)
                A(lgT, bank[5][:, 0:P], ACT.Copy).then_inc(lgT_copied, 1)

            def top_exp(t):
                act.wait_ge(mx_ready, t + 1)
                A(e4, e4, ACT.Exp, accum_out=sums[:, 0:1]).then_inc(ex_ready, 1)

            for n in range(2 * T):
                o_copy(n)
                if n == 2:
                    conf_rstd()
                    mixT_copy(0)
                if n == 3:
                    for j in range(CT):
                        act.wait_ge(cy_ready, j + 1)
                        own.mark(A(cacc[:, j, :], cacc[:, j, :], ACT.Identity, scale=PT[:, j, 32:33],
                                   bias=PT[:, j, 33:34]))
                    for j in range(CT):
                        act.wait_ge(act_self, own.n - CT + j + 1)
                        A(ubuf[:, j, 0:SEQ], cacc[:, j, :], ACT.Tanh).then_inc(cth_ready, 1)
                    act.preload_act_table_set("natural_log_exp_and_others")
                if n == 4:
                    mixT_copy(1)
                if n % 2 == 1:
                    o_rstd(n // 2)
            act.dma_start(bdn, b_down[0]).then_inc(bias_in, 16)
            mixT_copy(2)
            act.wait_ge(mix_ready, T)
            x2_rstd(0)
            xnT_copy(0)
            x2_rstd(1)
            lgT_copy(0)
            mixT_copy(3)
            for t in range(1, T):
                xnT_copy(t)
                if t + 1 < T:
                    lgT_copy(t)
                    top_exp(t - 1)
                    x2_rstd(t + 1)
                else:
                    top_exp(t - 1)
                    lgT_copy(t)
            top_exp(T - 1)

            act.wait_ge(gt_done, 1)
            A(GT, bank[7][0:E, :], ACT.Copy).then_inc(gt_copied, 1)

            def xT_copy(v):
                act.wait_ge(xt_done, v)
                A(xT[:, 0:2, :, :], view(bank[6], 0, 2, 2, P), ACT.Copy)
                A(xT[:, 2:4, :, :], view(bank[7], 0, 2, 2, P), ACT.Copy).then_inc(xt_ready, 1)

            xT_copy(1)
            act.wait_ge(route_ready, 1)
            m = visits_less_two(act)

            def hid_copy():
                for g in range(GROUPS):
                    A(hid[:, g, :], bank[g][:, :], ACT.Copy).then_inc(hid_ready, 1)



            def results(stage):
                for g in range(GROUPS):
                    ins = A(yb[:, g, :], bank[4 + g // 2][:, (g % 2) * QD:(g % 2 + 1) * QD], ACT.Copy,
                            scale=slot_gate[:, stage, g:g + 1])
                ins.then_inc(y_ready, 1)

            def sigmoid_gate(visit):
                act.wait_ge(g2_ready, visit)
                A(sg, g2, ACT.Sigmoid, scale=ALPHA).then_inc(sg_ready, 1)

            act.sem_inc(y_ready, 1)
            act.wait_ge(gu_used, KC)
            hid_copy()
            xT_copy(2)
            sigmoid_gate(1)
            with act.Fori(1, m + 2) as i:
                act.wait_ge(gu_used, i * KC + KC)
                act.wait_ge(ht_done, i * 2)
                hid_copy()
                xT_copy(i + 2)
                sigmoid_gate(i + 1)
                act.wait_ge(d_used, i * 4 + 4)
                act.wait_ge(idx_ready, i + 3)
                act.wait_ge(landed, i)
                results(3)
            act.wait_ge(d_used, m * 4 + 12)
            act.wait_ge(landed, m + 2)
            results(2)
            act.dma_start(finw, final_norm_w.rearrange("(o d) -> o d", o=1).to_broadcast([P, D])).then_inc(
                late_in, 16)
            act.preload_act_table_set("natural_log_exp_and_others")
            for t in range(T):
                act.wait_ge(fin_in[t], 16)
                A(zrows[:, (t % 2) * D:(t % 2 + 1) * D], fin[:, t, :], ACT.Square, accum_out=ssx[:, t:t + 1]
                  ).then_inc(fss_ready, 1)
                act.wait_ge(fss_ready, 3 * t + 1)
                A(ssx[:, t:t + 1], ssx[:, t:t + 1], ACT.Ln, bias=epst, scale=1.0 / D).then_inc(fss_ready, 1)
                act.wait_ge(fss_ready, 3 * t + 2)
                A(rstdx[:, t:t + 1], ssx[:, t:t + 1], ACT.Exp, scale=-0.5).then_inc(fss_ready, 1)

        @block.vector
        def _(dve):
            own = Own(dve, dve_self)
            V = nc.vector
            bcm = lambda m: m.rearrange("p (o c) -> p o c", o=1).to_broadcast([P, T, P])

            dve.wait_ge(params_turned, 1)
            own.mark(V.tensor_copy(PT[:, :, 0:50], view(bank[3], 0, CT, 64)[:, :, 0:50]))
            own.settle()
            own.mark(V.tensor_scalar(PT[:, :, 0:TAPS], PT[:, :, 0:TAPS], 0.5, None, ALU.mult))
            own.mark(V.tensor_scalar(PT[:, :, 32:34], PT[:, :, 32:34], 0.5, None, ALU.mult))
            own.settle()
            dve.sem_inc(params_ready, 1)
            for t in range(T):
                dve.wait_ge(rstdx_ready, t + 1)
                V.tensor_scalar(xr[:, t, :], xr[:, t, :], rstdx[:, t:t + 1], None, ALU.mult).then_inc(xs_ready, 1)
            for c in range(1, KC, 2):
                dve.wait_ge(x_turned, c + 1)
                V.tensor_scalar(hT[:, c, :], bank[c][:, :], PT[:, c % CT, 46 + c // CT:47 + c // CT], None,
                                ALU.mult).then_inc(h_dve, 1)
            dve.wait_ge(ab_turned, 1)
            dve.wait_ge(gate_in, 48)
            own.mark(V.tensor_tensor(ym, view(bank[4], 0, T, 2 * H)[:, :, H:2 * H],
                                     dtb.rearrange("p (o h) -> p o h", o=1).to_broadcast([P, T, H]), ALU.add))
            own.settle()
            V.scalar_tensor_tensor(out=ya, in0=ym, scalar=-1.0, in1=ym, op0=ALU.mult, op1=ALU.max
                                   ).then_inc(ab_dve, 1)
            dve.wait_ge(ab_act, 1)
            own.mark(V.tensor_scalar(beta, thb, 0.5, 0.5, ALU.mult, ALU.add))
            own.mark(V.tensor_scalar(ym, ym, 0.0, None, ALU.max))
            own.settle()
            own.mark(V.tensor_scalar(betah, beta, 0.5, None, ALU.mult))
            dve.wait_ge(ab_act, 2)
            own.mark(V.tensor_tensor(ym, ym, yl, ALU.add))
            own.settle()
            V.scalar_tensor_tensor(out=gg, in0=ym, scalar=-1.0,
                                   in1=nA.rearrange("p (o h) -> p o h", o=1).to_broadcast([P, T, H]),
                                   op0=ALU.mult, op1=ALU.mult).then_inc(g_ready, 1)
            dve.wait_ge(gsum_done, 1)
            own.mark(V.tensor_copy(gc, view(bank[4], 64, T, H)))
            own.settle()
            own.mark(V.tensor_tensor(kts, view(bank[4], 96, T, H), gc, ALU.subtract))
            own.settle()
            dve.sem_inc(gc_ready, 1)
            dve.wait_ge(ab_act, 3)
            V.tensor_tensor(ge, beta, eg, ALU.mult).then_inc(ga_ready, 1)

            def cf_value(j):
                dve.wait_ge(proj_act, j + 1)
                V.scalar_tensor_tensor(out=ubuf[:, j, PAD:], in0=th[j % 2], scalar=1.0,
                                       in1=bank_of(2 * j)[:, :], op0=ALU.add, op1=ALU.mult
                                       ).then_inc(proj_dve, 1)

            tap_at = [0]

            def taps(n, j_max):
                for _ in range(n):
                    j, k = divmod(tap_at[0], TAPS)
                    if j > j_max or j >= CT:
                        return
                    if k == 0:
                        dve.wait_ge(proj_dve, j + 1)
                        own.mark(V.tensor_scalar(cacc[:, j, :], ubuf[:, j, 0:SEQ], PT[:, j, 0:1],
                                                 PT[:, j, TAPS:TAPS + 1], ALU.mult, ALU.add))
                    else:
                        own.settle()
                        own.mark(V.scalar_tensor_tensor(out=cacc[:, j, :], in0=ubuf[:, j, k:k + SEQ],
                                                        scalar=PT[:, j, k:k + 1], in1=cacc[:, j, :],
                                                        op0=ALU.mult, op1=ALU.add))
                    tap_at[0] += 1
                    if k == TAPS - 1:
                        own.settle()
                        dve.sem_inc(cacc_ready, 1)

            def conv4(s):
                kind, h, b = TILES[s]
                if kind != "qkv":
                    return
                i = 3 * h + b
                dst = (qT[h % 2], kT[h % 2], vT)[b]
                dve.wait_ge(proj_act, CT + i + 1)
                if b < 2 and h >= 2:
                    dve.wait_ge(qk_done, h - 1)
                    dve.wait_ge(kv_turned, h - 1)
                if b == 2 and h >= 1:
                    dve.wait_ge(kv_turned, h)
                w = lambda k: PT[:, h, 34 + 3 * k + b:35 + 3 * k + b]
                own.mark(V.tensor_scalar(dst, preb[i % 2][:, 0:SEQ], w(0), None, ALU.mult))
                for k in range(1, CONV):
                    own.settle()
                    ins = V.scalar_tensor_tensor(out=dst, in0=preb[i % 2][:, k:k + SEQ], scalar=w(k), in1=dst,
                                                 op0=ALU.mult, op1=ALU.add)
                    if k < CONV - 1:
                        own.mark(ins)
                ins.then_inc(conv_ready, 1)

            def silu(s):
                kind, h, b = TILES[s]
                if kind == "z":
                    dve.wait_ge(proj_act, CT + 3 * H + h + 1)
                    V.scalar_tensor_tensor(out=zr[:, h, :], in0=th[1], scalar=1.0, in1=bank_of(s)[:, :],
                                           op0=ALU.add, op1=ALU.mult).then_inc(proj_dve, 1)
                if kind != "qkv":
                    return
                i = 3 * h + b
                dst = (qT[h % 2], kT[h % 2], vT)[b]
                dve.wait_ge(tanh_ready, i + 1)
                V.scalar_tensor_tensor(out=dst, in0=th[1], scalar=1.0, in1=dst, op0=ALU.add,
                                       op1=ALU.mult).then_inc(silu_ready, 1)

            def norm(s):
                kind, h, b = TILES[s]
                if kind != "qkv" or b == 2:
                    return
                dst = (qT[h % 2], kT[h % 2])[b]
                dve.wait_ge(rs_ready, 2 * h + b + 1)
                V.scalar_tensor_tensor(out=dst, in0=dst, scalar=0.5 * (DK ** -0.5 if b == 0 else 1.0),
                                       in1=sq[b], op0=ALU.mult, op1=ALU.mult).then_inc(norm_ready, 1)

            def level(h, s):
                if s == 1:
                    dve.wait_ge(p_done, 6 * h + 1)
                    own.mark(V.tensor_tensor(Pm, view(bank[5], 0, T, P), bcm(lmask[1]), ALU.mult))
                    own.settle()
                    V.scalar_tensor_tensor(out=XT, in0=Pm, scalar=-1.0, in1=bcm(ident), op0=ALU.mult,
                                           op1=ALU.add).then_inc(xx_ready, 1)
                    return
                dve.wait_ge(p_done, 6 * h + LEVELS.index(s) + 1)
                V.tensor_tensor(Pm, view(bank[5], 0, T, P), bcm(lmask[s]), ALU.mult).then_inc(p_ready, 1)

            def level_x(h, s):
                k = LEVELS.index(s)
                dve.wait_ge(xx_done, 5 * h + k)
                V.tensor_tensor(XT, XT, view(bank[7], 0, T, P), ALU.subtract).then_inc(xx_ready, 1)
                if s < LEVELS[-1]:
                    V.tensor_tensor(X, X, view(bank[6], 0, T, P), ALU.subtract).then_inc(xx_ready, 1)

            def gdn(h, k):
                if k == 0:
                    dve.wait_ge(gcb_done, h + 1)
                    if h >= 1:
                        dve.wait_ge(uw_done, h)
                    own.mark(V.tensor_tensor(DT, view(bank[7], 0, T, P),
                                             gc[:, :, h:h + 1].to_broadcast([P, T, P]), ALU.subtract))
                    own.settle()
                    V.tensor_scalar(Dm, DT, -1.0, 0.0, ALU.mult, ALU.min).then_inc(diff_ready, 1)
                    dve.wait_ge(diff_ready, 2 * h + 1)
                    V.tensor_scalar(DT, DT, 0.0, None, ALU.min).then_inc(diff_ready, 1)
                if k == 1:
                    dve.wait_ge(egb_ready, h + 1)
                    if h == 0:
                        dve.wait_ge(bias_ready, 1)
                    q = qT[h % 2].rearrange("p (t f c) -> p t f c", t=T, f=2)
                    e = th[0].rearrange("p (t f c) -> p t f c", t=T, f=2)
                    d = wqT[:, h, :, :].rearrange("p (t f) c -> p t f c", f=2)
                    own.mark(V.tensor_tensor(d[:, :, 0, CHUNK:P], q[:, :, 0, :], e[:, :, 0, :], ALU.mult))
                    own.mark(V.tensor_tensor(d[:, :, 1, 0:CHUNK], q[:, :, 1, :], e[:, :, 1, :], ALU.mult))
                    own.settle()
                    dve.sem_inc(qd_ready, 1)
                if k == 2:
                    dve.wait_ge(dmask_ready, 2 * h + 1)
                    dve.wait_ge(kk_done, h + 1)
                    for t in range(T):
                        ins = V.scalar_tensor_tensor(out=Am[:, t, :], in0=view(bank[5], 0, T, P)[:, t, :],
                                                     scalar=beta[:, t, h:h + 1], in1=Dm[:, t, :], op0=ALU.mult,
                                                     op1=ALU.mult)
                    ins.then_inc(a_ready, 1)
                    dve.wait_ge(dmask_ready, 2 * h + 2)
                    dve.wait_ge(qk_done, h + 1)
                    if h == 0:
                        dve.wait_ge(zero_out, 32)
                    V.tensor_tensor(intraT[:, h, :, :], view(bank[6], 0, T, P), DT, ALU.mult
                                    ).then_inc(in_ready, 1)
                    dve.wait_ge(a_ready, h + 1)
                    own.mark(V.tensor_tensor(X, Am, bcm(lmask1t), ALU.mult))
                    own.settle()
                    V.scalar_tensor_tensor(out=X, in0=X, scalar=-1.0, in1=bcm(ident), op0=ALU.mult,
                                           op1=ALU.add).then_inc(xx_ready, 1)
                if k == 3:
                    dve.wait_ge(kv_turned, h + 1)
                    bct = lambda v: v[:, :, h:h + 1].to_broadcast([P, T, P])
                    own.mark(V.tensor_tensor(kbgv, view(bank[3], 0, T, P), bct(ge), ALU.mult))
                    own.mark(V.tensor_tensor(ktail[:, h, :, :], view(bank[3], 0, T, P), bct(kts), ALU.mult))
                    own.mark(V.tensor_tensor(uval[:, h, :, :], view(bank[4], 0, T, P), bct(betah), ALU.mult))
                    own.settle()
                    dve.sem_inc(kv_ready, 1)
                if k == 4:
                    level(h, 1)
                if 5 <= k < 15:
                    s = LEVELS[1 + (k - 5) // 2]
                    if k % 2 == 1:
                        level(h, s)
                    else:
                        level_x(h, s)

            dve.wait_ge(masks_ready, 1)
            own.mark(V.tensor_copy(tri16, trif))
            own.mark(V.tensor_copy(ones16, ones))
            for s in range(NT + 1):
                h, steps = gdn_of(s)
                p = s - 1
                if 1 <= s <= 2 * CT and s % 2 == 0:
                    cf_value(s // 2 - 1)
                jobs = []
                tap = lambda n: (lambda: taps(n, CT - 1 if s >= Q0 else (s - 2) // 2))
                if p >= 0:
                    jobs += [tap(2) if p >= Z0 else lambda: conv4(p), lambda: None, lambda: silu(p)]
                if s >= 2:
                    if 0 in steps:
                        steps = [0, 1, 2, 4, 3]
                        jobs = [jobs[0], lambda: None, lambda: None, jobs[2], lambda: norm(s - 2), tap(1)]
                    elif steps:
                        jobs[1] = tap(1)
                        jobs += [tap(1), tap(1), lambda: norm(s - 2), tap(3)]
                    else:
                        jobs += [tap(4), lambda: norm(s - 2), tap(3)]
                for n in range(max(len(steps), len(jobs))):
                    if n < len(steps):
                        gdn(h, steps[n])
                    if n < len(jobs):
                        jobs[n]()
            while tap_at[0] < CT * TAPS:
                taps(1, CT)

            def conf_center():
                dve.wait_ge(mean_done, 1)
                for j in range(CT):
                    V.scalar_tensor_tensor(out=cacc[:, j, :], in0=bank[1][:, :], scalar=-1.0 / CF,
                                           in1=cacc[:, j, :], op0=ALU.mult, op1=ALU.add).then_inc(xc_ready, 1)

            def router_scale():
                dve.wait_ge(wr_in, 48)
                for r in range(2):
                    ins = V.tensor_tensor(router[:, CT * r:CT * (r + 1), :], router[:, CT * r:CT * (r + 1), :],
                                          PT[:, :, 48 + r:49 + r].to_broadcast([P, CT, E]), ALU.mult)
                ins.then_inc(router_ready, 1)

            def conf_scale():
                dve.wait_ge(crs_ready, 1)
                for j in range(CT):
                    dve.wait_ge(csq_ready, j + 1)
                    V.tensor_tensor(cacc[:, j, :], cacc[:, j, :], vbuf[:, :], ALU.mult).then_inc(cy_ready, 1)



            def conf_silu():
                for j in range(CT):
                    dve.wait_ge(cth_ready, j + 1)
                    V.scalar_tensor_tensor(out=cacc[:, j, :], in0=ubuf[:, j, 0:SEQ], scalar=1.0,
                                           in1=cacc[:, j, :], op0=ALU.add, op1=ALU.mult).then_inc(cmix_ready, 1)

            def z_weight():
                dve.wait_ge(late_in, 16)
                dve.wait_ge(proj_dve, CT + T)
                for t in range(T):
                    zt = zr[:, t, :].rearrange("p (h c) -> p h c", h=H)
                    own.mark(V.scalar_tensor_tensor(
                        out=zt, in0=zt, scalar=0.5,
                        in1=normrow.rearrange("p (o c) -> p o c", o=1).to_broadcast([P, H, P]),
                        op0=ALU.mult, op1=ALU.mult))

            def rec(n):
                t, f = divmod(n, 2)
                b = CHUNK * f
                if n == 0:
                    dve.wait_ge(su_done, 1)
                    V.tensor_copy(S, view(bank[5], 0, H, P)).then_inc(s_ready, H)
                    return
                dve.wait_ge(ws_done, n)
                V.tensor_tensor(vn[b:b + CHUNK, :, :], uval[b:b + CHUNK, :, t, :],
                                view(bank[3 + n % 2], 0, H, P)[b:b + CHUNK, :, :], ALU.subtract
                                ).then_inc(vn_ready, 1)
                dve.wait_ge(su_done, n + 1)
                for h in range(H):
                    V.scalar_tensor_tensor(out=S[:, h, :], in0=S[:, h, :],
                                           scalar=gtB[:, f, t * H + h:t * H + h + 1],
                                           in1=view(bank[5], 0, H, P)[:, h, :], op0=ALU.mult,
                                           op1=ALU.add).then_inc(s_ready, 1)

            def gated(t):
                dve.wait_ge(osq_ready, t + 1)
                V.tensor_reduce(rso, osq, AX_X, ALU.add).then_inc(oss_ready, 1)
                dve.wait_ge(ors_ready, t + 1)
                o = osb[t % 2]
                own.mark(V.tensor_tensor(o, o, rsl.rearrange("p (h o) -> p h o", o=1).to_broadcast([P, H, P]),
                                         ALU.mult))
                own.settle()
                V.tensor_tensor(o, o, zr[:, t, :].rearrange("p (h c) -> p h c", h=H), ALU.mult
                                ).then_inc(mix_ready, 1)

            def residual(t):
                pair = PAIRS[t % 2]
                dve.wait_ge(op_done, t + 1)
                dve.wait_ge(xres_in[t], 16)
                own.mark(V.tensor_tensor(x2[:, t, 0:HALF], pair[0][:, :], x2[:, t, 0:HALF], ALU.add))
                own.mark(V.tensor_tensor(x2[:, t, HALF:D], pair[1][:, :], x2[:, t, HALF:D], ALU.add))
                own.settle()
                dve.sem_inc(x2_ready, 1)

            def normed(t):
                dve.wait_ge(rstd2_ready, t + 1)
                if t >= 2:
                    dve.wait_ge(xn_out[t % 2], 16 * (t // 2))
                if t == 0:
                    dve.wait_ge(zero_out, 32)
                    dve.wait_ge(wr_in, 48)
                V.scalar_tensor_tensor(out=xn[:, t % 2, :], in0=x2[:, t, :], scalar=rstd2[:, t:t + 1],
                                       in1=ffnw[:, :], op0=ALU.mult, op1=ALU.mult).then_inc(xn_ready, 1)

            def route(t):
                dve.wait_ge(lg_done, t + 1)
                own.mark(V.tensor_reduce(lg, bank[6][:, 0:P].rearrange("p (j e) -> p e j", j=4), AX_X,
                                         ALU.add))
                own.settle()
                own.mark(V.scalar_tensor_tensor(out=lg, in0=lg, scalar=rstd2[:, t:t + 1], in1=bro, op0=ALU.mult,
                                                op1=ALU.add))
                own.settle()
                own.mark(V.max(m8, lg))
                own.settle()
                own.mark(V.max_index(i8.bitcast(mybir.dt.uint32), m8, lg))
                own.mark(V.tensor_scalar(e4, m8[:, 0:TOP_K], m8[:, 0:1], None, ALU.subtract))
                own.settle()
                dve.sem_inc(mx_ready, 1)
                own.mark(V.tensor_copy(pr4, i8.bitcast(mybir.dt.uint32)[:, 0:TOP_K]))
                dve.wait_ge(ex_ready, t + 1)
                own.mark(V.reciprocal(sums[:, 1:2], sums[:, 0:1]))
                own.settle()
                own.mark(V.tensor_scalar(e4, e4, sums[:, 1:2], None, ALU.mult))
                own.settle()
                own.mark(V.tensor_scalar(Gm[:, t, :], iota_e, pr4[:, 0:1], e4[:, 0:1], ALU.is_equal, ALU.mult))
                for k in range(1, TOP_K):
                    own.mark(V.tensor_scalar(lg, iota_e, pr4[:, k:k + 1], e4[:, k:k + 1], ALU.is_equal,
                                             ALU.mult))
                    own.settle()
                    own.mark(V.tensor_tensor(Gm[:, t, :], Gm[:, t, :], lg, ALU.add))
                    own.settle()
                V.tensor_scalar(Msk[:, t, :], Gm[:, t, :], 0.0, None, ALU.is_gt).then_inc(gate_ready, 1)

            rec(0)
            conf_center()
            rec(1)
            z_weight()
            rec(2)
            gated(0)
            rec(3)
            conf_scale()
            rec(4)
            conf_silu()
            gated(1)
            rec(5)
            router_scale()
            rec(6)
            gated(2)
            residual(0)
            rec(7)
            gated(3)
            normed(0)
            residual(1)
            normed(1)
            route(0)
            residual(2)
            normed(2)
            route(1)
            residual(3)
            normed(3)
            route(2)
            route(3)
            own.mark(V.memset(idx[:, :], 0))
            own.mark(V.memset(slot_gate, 0.0))
            tgv = view(tg, 0, T * E, 6)
            for t in range(T):
                own.mark(V.memset(tgv[:, t * E:(t + 1) * E, 0:1], float(t * P)))
            own.mark(V.tensor_copy(tgv[:, :, 1:2], tokp.rearrange("p (a b) -> p a b", a=1).to_broadcast(
                [P, T * E, 1])))
            own.mark(V.memset(tgv[:, :, 2:3], 1.0))
            gflat = view(kbg, 0, T * E, 1)
            gr = view(kbg, 2 * T * E + 8, T * E, 1)
            own.mark(V.tensor_copy(tgv[:, :, 3:4], gflat))
            own.settle()
            own.mark(V.tensor_tensor(gr, gflat, tgv[:, :, 3:4], ALU.subtract))
            own.settle()
            own.mark(V.tensor_copy(tgv[:, :, 4:5], gr))
            own.settle()
            own.mark(V.tensor_tensor(gr, gr, tgv[:, :, 4:5], ALU.subtract))
            own.settle()
            own.mark(V.tensor_copy(tgv[:, :, 5:6], gr))
            dve.wait_ge(pos_done, 1)
            pv = view(bank[6], 0, T, E)
            own.mark(V.tensor_tensor(pos, Msk, pv, ALU.mult))
            own.mark(V.tensor_copy(cnt, bank[6][:, T * E:T * E + E]))
            own.settle()
            own.mark(V.tensor_scalar(pos, pos, -1.0, None, ALU.add))
            own.settle()

            ohv = view(onehot, 0, T, GROUPS * P)

            def hot(e):
                for t in range(T):
                    V.tensor_scalar(ohv[:, t, :], slot_no[:, :], pos[:, t, bass.ds(e, 1)], None,
                                    ALU.is_equal).then_inc(hot_ready, 1)

            def lower(e):
                V.tensor_scalar(pos[:, :, bass.ds(e, 1)], pos[:, :, bass.ds(e, 1)], float(-CAP), None,
                                ALU.add).then_inc(hot_ready, 1)

            iv = idx[:, :].rearrange("p (s g) -> p s g", s=STAGES)
            STEPS_IDX = 13

            def numbers(base, shift=True):
                ps = bank[6][:, 0:GROUPS * 6].rearrange("p (g c) -> p g c", c=6)
                s = own.s
                c = base

                def mk(ins):
                    nonlocal c
                    ins.then_inc(s, 1)
                    c = c + 1

                for k in range(STAGES - 1 if shift else 0, 0, -1):
                    mk(V.tensor_copy(iv[:, k, :], iv[:, k - 1, :]))
                    mk(V.tensor_copy(slot_gate[:, k, :], slot_gate[:, k - 1, :]))
                    if k > 1:
                        dve.wait_ge(s, c)
                mk(V.tensor_tensor(tix[:, 0, :], slotbase, ps[:, :, 2], ALU.mult))
                mk(V.tensor_reduce(tix[:, 1, :], ps[:, :, 0:2], AX_X, ALU.add))
                dve.wait_ge(s, c)
                mk(V.tensor_reduce(slot_gate[:, 0, :], ps[:, :, 3:6], AX_X, ALU.add))
                mk(V.tensor_tensor(tix[:, 2, :], tix[:, 1, :], tix[:, 0, :], ALU.subtract))
                dve.wait_ge(s, c)
                mk(V.tensor_tensor(tix[:, 3, :], tix[:, 2, :], slotbase, ALU.add))
                dve.wait_ge(s, c)
                mk(V.tensor_scalar(tix[:, 0, :], tix[:, 3, :], 4.0, jcol[:, 0:1], ALU.mult, ALU.add))
                dve.wait_ge(s, c)
                mk(V.tensor_copy(iv[:, 0, :], tix[:, 0, :]))
                dve.wait_ge(s, c)
                dve.sem_inc(idx_ready, 1)

            hot(0)
            dve.wait_ge(hot_ready, T)
            lower(0)
            dve.wait_ge(idx_done, 1)
            numbers(own.n, shift=False)
            own.n += STEPS_IDX - 2 * (STAGES - 1)
            own.mark(V.tensor_reduce(rnd[:, 0:1], cnt, AX_X, ALU.max))
            own.settle()
            own.mark(V.tensor_scalar(rnd[:, 1:1 + ROUNDS_MAX - 1], thr, rnd[:, 0:1], None, ALU.is_lt))
            own.settle()
            own.mark(V.tensor_reduce(rnd[:, 7:8], rnd[:, 1:1 + ROUNDS_MAX - 1], AX_X, ALU.add))
            own.settle()
            own.mark(V.tensor_scalar(n_iter[:, 0:1], rnd[:, 7:8], float(E), float(E - 2), ALU.mult, ALU.add))
            for r in range(ROUNDS_MAX):
                own.settle()
                own.mark(V.tensor_scalar(leftf, cnt, float(-r * CAP), 0.0, ALU.add, ALU.max))
                own.settle()
                own.mark(V.tensor_copy(left[:, r * E:(r + 1) * E], leftf))
            own.mark(V.memset(left[:, ROUNDS_MAX * E:], 0))
            own.settle()
            dve.sem_inc(route_ready, 1)
            hot(1)
            dve.wait_ge(hot_ready, 2 * T + 1)
            lower(1)
            dve.wait_ge(idx_done, 2)
            dve.wait_ge(gathered, 16 * GROUPS)
            numbers(own.n)
            own.n += STEPS_IDX
            hot(2)
            dve.wait_ge(hot_ready, 3 * T + 2)
            lower(2)
            for t in range(T):
                dve.wait_ge(bd_done, t + 1)
                V.tensor_tensor(x2[:, t, 0:HALF], bank[4][:, :], x2[:, t, 0:HALF], ALU.add)
                V.tensor_tensor(x2[:, t, HALF:D], bank[5][:, :], x2[:, t, HALF:D], ALU.add
                                ).then_inc(acc_ready, 1)
            m = visits_less_two(dve)
            dve.wait_ge(idx_done, 3)
            dve.wait_ge(gathered, 32 * GROUPS)
            numbers(own.n)
            own.n += STEPS_IDX
            hot(3)
            dve.wait_ge(hot_ready, 4 * T + 3)
            lower(3)

            def act_part(e, visit, base):
                s = own.s
                c = base
                dve.wait_ge(ht_done, visit * 2 - 1)

                def bias(half):
                    v = bgu[:, half * KC:(half + 1) * KC, bass.ds(e, 1)]
                    return v.rearrange("p (j hh) o -> p hh j (o)", hh=2).to_broadcast([P, 2, 4, GROUP])

                def four(v):
                    return v.rearrange("p hh (j s) -> p hh j s", j=4)

                src = [view(bank[6 + g // 2], (g % 2) * 256, 2, P) for g in range(GROUPS)]
                for g in range(GROUPS):
                    V.tensor_tensor(four(g2[:, g, :, :]), four(src[g]), bias(0), ALU.add).then_inc(s, 1)
                c = c + GROUPS
                dve.wait_ge(s, c)
                dve.sem_inc(half_read, 1)
                V.tensor_scalar(g2, g2, LIMIT, None, ALU.min).then_inc(g2_ready, 1)
                dve.wait_ge(ht_done, visit * 2)
                for g in range(GROUPS):
                    V.tensor_tensor(four(u2[:, g, :, :]), four(src[g]), bias(1), ALU.add).then_inc(s, 1)
                c = c + GROUPS
                dve.wait_ge(s, c)
                dve.sem_inc(half_read, 1)
                V.tensor_scalar(u2, u2, LIMIT, -LIMIT, ALU.min, ALU.max).then_inc(s, 1)
                c = c + 1
                dve.wait_ge(sg_ready, visit)
                V.tensor_tensor(g2, g2, sg, ALU.mult).then_inc(s, 1)
                c = c + 1
                dve.wait_ge(s, c)
                dve.wait_ge(d_used, visit * 4)
                flat = lambda v: v.rearrange("p g hh n -> p (g hh n)")
                V.scalar_tensor_tensor(out=flat(actT), in0=flat(u2), scalar=1.0, in1=flat(g2), op0=ALU.add,
                                       op1=ALU.mult).then_inc(act_ready, 1)

            STEPS_ACT = 2 * GROUPS + 2
            LOOP_OWN = STEPS_IDX + STEPS_ACT
            act_part(0, 1, own.n)
            own.n += STEPS_ACT
            with dve.Fori(1, m + 2) as i:
                base = (i - 1) * LOOP_OWN + own.n
                dve.wait_ge(idx_done, i + 3)
                dve.wait_ge(gathered, i * (16 * GROUPS) + 32 * GROUPS)
                dve.wait_ge(landed, i)
                dve.wait_ge(y_ready, i)
                numbers(base)
                e3 = (i + 3) % E
                hot(e3)
                dve.wait_ge(hot_ready, (i + 4) * (T + 1) - 1)
                lower(e3)
                act_part(i % E, i + 1, base + STEPS_IDX)
            dve.wait_ge(late_in, 32)
            for t in range(T):
                dve.wait_ge(fss_ready, 3 * t + 3)
                V.scalar_tensor_tensor(out=fin[:, t, :], in0=fin[:, t, :], scalar=rstdx[:, t:t + 1], in1=finw,
                                       op0=ALU.mult, op1=ALU.mult).then_inc(fin_ready, 1)

        @block.tensor
        def _(pe):
            M = nc.tensor.matmul
            TR = nc.tensor.transpose
            pe.wait_ge(consts_ready, 1)
            pe.wait_ge(param_in, 112)
            for j in range(CT):
                ins = TR(view(bank[3], 0, CT, 64)[:, j, 0:50], prow[0:50, j * P:(j + 1) * P], ident[0:50, 0:50])
            ins.then_inc(params_turned, 1)
            for t in range(T):
                pe.wait_ge(xs_ready, t + 1)
                if t == 0:
                    pe.wait_ge(params_ready, 1)

                for c in range(KC):
                    ins = TR(bank[c][:, t * P:(t + 1) * P], xr[:, t, c * P:(c + 1) * P], ident)
                    if t == T - 1:
                        ins.then_inc(x_turned, 1)
            pe.wait_ge(h_act, KC // 2)
            pe.wait_ge(h_dve, KC // 2)
            pe.wait_ge(gate_in, 48)
            for c in range(KC):
                ins = M(bank[3][0:2 * H, :], wab[:, c, :], hT[:, c, :], start=(c == 0), stop=(c == KC - 1))
            ins.then_inc(ab_done, 1)
            def bias_turn():
                pe.wait_ge(bias_in, 16)
                for j in range(2 * KC):
                    ins = TR(view(bank[5], 0, 2 * KC, E)[:, j, :], bgu_rows[:, j * P:(j + 1) * P], ident[0:E, 0:E])
                ins.then_inc(bias_turned, 1)

            def gates(k):
                if k == 0:
                    pe.wait_ge(ab_copied, 1)
                    for t in range(T):
                        ins = TR(view(bank[4], 0, T, 2 * H)[:, t, :], ab_sb[:, t * P:(t + 1) * P],
                                 ident[0:2 * H, 0:2 * H])
                    ins.then_inc(ab_turned, 1)
                else:
                    pe.wait_ge(g_ready, 1)
                    pe.wait_ge(masks_ready, 1)
                    g = gg.rearrange("p t h -> p (t h)")
                    M(bank[4][:, 64:64 + TH], triu, g, start=True, stop=True)
                    M(bank[4][:, 96:96 + TH], blk, g, start=True, stop=True)
                    M(bank[4][:, 128:128 + TH], half0, g, start=True, stop=True)
                    M(bank[4][:, 128 + TH:128 + 2 * TH], half1, g, start=True, stop=True
                      ).then_inc(gsum_done, 1)

            def free_bank(s):
                p = s - 3
                if p < 0:
                    return
                kind, a, b = TILES[p]
                if kind == "cf":
                    pe.wait_ge(proj_dve, a + 1)
                elif kind == "qkv":
                    pe.wait_ge(proj_act, CT + 3 * a + b + 1)
                else:
                    pe.wait_ge(proj_dve, CT + a + 1)

            def proj(s, c):
                kind, a, b = TILES[s]
                if c == 0:
                    free_bank(s)
                if kind == "z":
                    u = NU - 2 + c // 4
                    pe.wait_ge(slot_in[u % 8], 32)
                    ins = M(bank_of(s)[:, :], hT[:, c, a * P:(a + 1) * P], unit_ap(u)[:, c % 4, :],
                            start=(c == 0), stop=(c == KC - 1))
                else:
                    u, half = UNIT_OF[s]
                    pe.wait_ge(slot_in[u % 8], 16 * (u // 8 + 1))
                    ins = M(bank_of(s)[:, :], unit_ap(u)[:, c, half * P:(half + 1) * P], hT[:, c, :],
                            start=(c == 0), stop=(c == KC - 1))
                if c == KC - 1:
                    ins.then_inc(proj_done, 1)

            def ssum(i):
                h, b = divmod(i, 3)
                if b == 2:
                    return
                pe.wait_ge(sq_ready, 2 * h + b + 1)
                if h >= 1:
                    pe.wait_ge(kv_ready, h)
                elif b == 1:
                    pe.wait_ge(ga_ready, 1)
                if h >= 2:
                    pe.wait_ge(uw_ready, 3 * (h - 1))
                M(bank[3 + b][:, :], ones, sq[b], start=True, stop=True).then_inc(ssum_done, 1)

            def gdn(h, k):
                q, kk = qT[h % 2], kT[h % 2]
                if k == 0 and h == 0:
                    pe.wait_ge(bias_ready, 1)
                if k == 0:
                    if h >= 1:
                        pe.wait_ge(xx_ready, 11 * h)
                    for t in range(T):
                        ins = M(bank[7][:, t * P:(t + 1) * P], gg[:, t, h:h + 1].to_broadcast([P, P]), triu,
                                start=True, stop=True)
                    ins.then_inc(gcb_done, 1)
                if k == 1:
                    pe.wait_ge(norm_ready, 2 * h + 2)
                    for t in range(T):
                        c = slice(t * P, (t + 1) * P)
                        ins = M(bank[5][:, c], kk[:, c], kk[:, c], start=True, stop=True)
                    ins.then_inc(kk_done, 1)
                if k == 2:
                    for t in range(T):
                        c = slice(t * P, (t + 1) * P)
                        ins = M(bank[6][:, c], kk[:, c], q[:, c], start=True, stop=True)
                    ins.then_inc(qk_done, 1)
                if k == 3:
                    pe.wait_ge(silu_ready, 3 * h + 3)
                    pe.wait_ge(rs_ready, 2 * h + 2)
                    if h >= 1:
                        pe.wait_ge(uw_ready, 3 * h)
                    for t in range(T):
                        TR(bank[3][:, t * P:(t + 1) * P], kk[:, t * P:(t + 1) * P], ident)
                    for t in range(T):
                        ins = TR(bank[4][:, t * P:(t + 1) * P], vT[:, t * P:(t + 1) * P], ident)
                    ins.then_inc(kv_turned, 1)
                if k == 4:
                    pe.wait_ge(a_ready, h + 1)
                    for t in range(T):
                        ins = TR(bank[5][:, t * P:(t + 1) * P], Am[:, t, :], ident)
                    ins.then_inc(p_done, 1)
                if k == 5:
                    pe.wait_ge(in_ready, h + 1)
                    pe.wait_ge(egb_ready, h + 1)
                if 5 <= k < 15:
                    lv = 1 + (k - 5) // 2
                    s = LEVELS[lv]
                    if k % 2 == 1:
                        pe.wait_ge(xx_ready, 11 * h + 2 * lv)
                        for t in range(T):
                            ins = M(bank[5][:, t * P:(t + 1) * P], Am[:, t, :], XT[:, t, :], start=True, stop=True)
                        ins.then_inc(p_done, 1)
                    else:
                        pe.wait_ge(p_ready, 5 * h + lv)
                        if s < LEVELS[-1]:
                            for t in range(T):
                                M(bank[6][:, t * P:(t + 1) * P], Pm[:, t, :], X[:, t, :], start=True, stop=True)
                        for t in range(T):
                            ins = M(bank[7][:, t * P:(t + 1) * P], X[:, t, :], Pm[:, t, :], start=True,
                                    stop=True)
                        ins.then_inc(xx_done, 1)
                if k == 15:
                    pe.wait_ge(xx_ready, 11 * h + 11)
                    pe.wait_ge(kv_ready, h + 1)
                    pe.wait_ge(rs_ready, min(2 * (h + 1) + 2, 2 * H))
                    for t in range(T):
                        M(bank[3][:, t * P:(t + 1) * P], XT[:, t, :], uval[:, h, t, :], start=True, stop=True)
                    for t in range(T):
                        ins = M(bank[4][:, t * P:(t + 1) * P], kbgv[:, t, :], XT[:, t, :], start=True, stop=True)
                    ins.then_inc(uw_done, 1)

            AT = {0: (1, 3, 5, 7, 8), 5: (2, 4, 5, 7, 8), 10: (1, 2, 4, 5, 7, 8)}
            for s in range(NT):
                h, steps = gdn_of(s)
                at = AT[steps[0]] if steps else ()
                for c in range(KC):
                    proj(s, c)
                    if s == 0 and c == 1:
                        gates(0)
                    if s == 2 and c == 1:
                        gates(1)
                    if s == 4 and c == 1:
                        bias_turn()
                    if c == 3 and s >= Q0 + 2:
                        if TILES[s - 2][0] == "qkv":
                            ssum(s - 2 - Q0)
                    for n, a in enumerate(at):
                        if a == c + 1:
                            gdn(h, steps[n])
            def conf_mean():
                pe.wait_ge(cacc_ready, CT)
                pe.wait_ge(proj_dve, CT + T)
                for j in range(CT):
                    ins = M(bank[1][:, :], ones, cacc[:, j, :], start=(j == 0), stop=(j == CT - 1))
                ins.then_inc(mean_done, 1)

            def conf_var():
                pe.wait_ge(csq_ready, CT)
                for j in range(CT):
                    ins = M(bank[0][:, :], ones, ubuf[:, j, 0:SEQ], start=(j == 0), stop=(j == CT - 1))
                ins.then_inc(var_done, 1)

            def ws(n):
                pe.wait_ge(s_ready, H * n)
                if n >= 2:
                    pe.wait_ge(o_copied, n - 1)
                for h in range(H):
                    ins = M(bank[3 + n % 2][:, h * P:(h + 1) * P], wqT[:, h, n, :], S[:, h, :],
                            start=(h == 0), stop=False, skip_group_check=True)
                ins.then_inc(ws_done, 1)

            def su(n):
                t, f = divmod(n, 2)
                b = CHUNK * f
                ob = CHUNK - b
                if n == 0:
                    pe.wait_ge(uw_ready, 3 * H)
                    pe.wait_ge(qd_ready, H)
                    new = uval[:, :, 0, :]
                else:
                    pe.wait_ge(vn_ready, n)
                    new = vn
                for h in range(H):
                    ins = M(bank[5][:, h * P:(h + 1) * P], ktail[b:b + CHUNK, h, t, :], new[b:b + CHUNK, h, :],
                            start=True, stop=True)
                ins.then_inc(su_done, 1)
                for h in range(H):
                    ins = M(bank[3 + n % 2][ob:ob + CHUNK, h * P:(h + 1) * P],
                            intraT[b:b + CHUNK, h, t, b:b + CHUNK], new[b:b + CHUNK, h, :],
                            start=(n == 0 and h == 0), stop=True, skip_group_check=True)
                ins.then_inc(o_done, 1)

            def mix_turn(t):
                pe.wait_ge(mix_ready, t + 1)
                if t >= 1:
                    pe.wait_ge(mixT_ready, t)
                for h in range(H):
                    ins = TR(bank[6][:, h * P:(h + 1) * P], osb[t % 2][:, h, :], ident)
                ins.then_inc(mix_turned, 1)

            def outp(t, k0, k1):
                pair = PAIRS[t % 2]
                for k in range(k0, k1):
                    kc, half = divmod(k, 2)
                    c = (kc + H) % KC
                    if k == 0 and t >= 2:
                        pe.wait_ge(x2_ready, t - 1)
                    if k == 0 and t == 0:
                        pe.wait_ge(cmix_ready, CT)
                        pe.wait_ge(crs_ready, 1)
                        for i in range(4):
                            pe.wait_ge(slot_in[4 + i], 32)
                    if c == 0 and half == 0:
                        pe.wait_ge(mixT_ready, t + 1)
                    lhs = mixT[t % 2][:, c, :] if c < H else cacc[:, c - H, t * P:(t + 1) * P]
                    w = view(ring, (4 + c // 2) * SLOT, 2, D)[:, c % 2, half * HALF:(half + 1) * HALF]
                    ins = M(pair[half][:, :], lhs, w, start=(kc == 0), stop=(kc == KC - 1))
                if k1 == 16:
                    ins.then_inc(op_done, 1)

            def xn_turn(t):
                pe.wait_ge(x2_ready, t + 1)
                if t >= 1:
                    pe.wait_ge(xnT_ready, t)
                else:
                    pe.wait_ge(o_copied, 2 * T)
                for c in range(KC):
                    ins = TR(bank[3 + c // 4][:, (c % 4) * P:(c % 4 + 1) * P], x2[:, t, c * P:(c + 1) * P],
                             ident)
                ins.then_inc(xn_turned, 1)

            def logits(t):
                pe.wait_ge(xnT_ready, t + 1)
                if t == 0:
                    pe.wait_ge(s_ready, H * 2 * T)
                    pe.wait_ge(router_ready, 1)
                else:
                    pe.wait_ge(lgT_copied, t)
                for r in range(2):
                    for j in range(4):
                        c = 4 * r + j
                        ins = M(bank[5][E * j:E * (j + 1), 0:P], router[:, c, :], xnT[t % 2][:, c, :],
                                start=(r == 0), stop=(r == 1), skip_group_check=True)
                ins.then_inc(lgT_done, 1)

            def logits_turn(t):
                pe.wait_ge(lgT_copied, t + 1)
                if t == 0:
                    pe.wait_ge(mixT_ready, T)
                else:
                    pe.wait_ge(mx_ready, t)
                TR(bank[6][:, 0:P], lgT, ident).then_inc(lg_done, 1)

            su(0)
            conf_mean()
            ws(1)
            su(1)
            ws(2)
            su(2)
            conf_var()
            ws(3)
            mix_turn(0)
            su(3)
            ws(4)
            su(4)
            outp(0, 0, 4)
            ws(5)
            outp(0, 4, 8)
            mix_turn(1)
            su(5)
            outp(0, 8, 12)
            ws(6)
            outp(0, 12, 16)
            su(6)
            outp(1, 0, 4)
            ws(7)
            outp(1, 4, 8)
            mix_turn(2)
            su(7)
            outp(1, 8, 16)
            outp(2, 0, 8)
            xn_turn(0)
            outp(2, 8, 16)
            mix_turn(3)
            logits(0)
            outp(3, 0, 4)
            logits_turn(0)
            outp(3, 4, 8)
            xn_turn(1)
            outp(3, 8, 12)
            logits(1)
            outp(3, 12, 16)
            logits_turn(1)
            for t in (2, 3):
                xn_turn(t)
                logits(t)
                logits_turn(t)
            pe.wait_ge(gate_ready, T)
            for t in range(T):
                for u in range(t + 1):
                    M(bank[6][:, t * E:(t + 1) * E], tri16 if u == t else ones16, Msk[:, u, :], start=(u == 0),
                      stop=(u == t))
            for u in range(T):
                ins = M(bank[6][:, T * E:(T + 1) * E], ones16, Msk[:, u, :], start=(u == 0), stop=(u == T - 1))
            ins.then_inc(pos_done, 1)

            ohv = view(onehot, 0, T, GROUPS, P)
            tgv = view(tg, 0, T, E, 6)

            def idx_mm(e, hot_wait):
                pe.wait_ge(hot_ready, hot_wait)
                for g in range(GROUPS):
                    for t in range(T):
                        ins = M(bank[6][:, 6 * g:6 * g + 6], ohv[:, t, g, :],
                                tgv[:, t, bass.ds(e, 1), :].rearrange("p o c -> p (o c)"),
                                start=(t == 0), stop=(t == T - 1))
                ins.then_inc(idx_done, 1)

            def xt_turn(g_wait):
                pe.wait_ge(gathered, g_wait)
                for g in range(GROUPS):
                    for hh in range(2):
                        b = bank[6 + g // 2]
                        c = (g % 2) * 256 + hh * P
                        ins = TR(b[:, c:c + P], xg[:, g, hh * P:(hh + 1) * P], ident)
                ins.then_inc(xt_done, 1)

            for t in range(T):
                ins = TR(bank[7][0:E, t * P:(t + 1) * P], Gm[:, t, :], ident)
            ins.then_inc(gt_done, 1)
            idx_mm(0, T)
            pe.wait_ge(idx_ready, 1)
            pe.wait_ge(gt_copied, 1)
            xt_turn(16 * GROUPS)
            pe.wait_ge(route_ready, 1)
            m = visits_less_two(pe)
            pe.sem_inc(d_used, 4)

            def routed_bias(t):
                if t == 0:
                    pe.wait_ge(bias_in, 32)
                else:
                    pe.wait_ge(acc_ready, t)
                for half in range(2):
                    ins = M(bank[4 + half][:, :], GT[:, t * P:(t + 1) * P], bdn[:, half * HALF:(half + 1) * HALF],
                            start=True, stop=True)
                ins.then_inc(bd_done, 1)

            def gate_up(i, groups=GROUPS, first=False):
                for c in range(KC):
                    pe.wait_ge(slot_in[c], i * 16 + 48)
                    w = view(ring, c * SLOT, 2, D)
                    for g in range(groups):
                        for j in range(4):
                            ins = M(bank[g][GROUP * j:GROUP * (j + 1), :],
                                    xT[:, g, c % 2, (c // 2) * GROUP:(c // 2 + 1) * GROUP],
                                    w[:, :, j * QD:(j + 1) * QD], start=(c == 0), stop=(c == KC - 1))
                    ins.then_inc(gu_used, 1)
                    if first and c == 0:
                        idx_mm(1, 2 * T + 1)
                    if first and 1 <= c <= T:
                        routed_bias(c - 1)
                    if first and c == 6:
                        pe.wait_ge(idx_ready, 2)
                        idx_mm(2, 3 * T + 2)
                    if not first and c == 5:
                        pe.wait_ge(half_read, i * 2)
                        idx_mm((i + 2) % E, (i + 3) * (T + 1) - 1)

            def down(i, groups, units, last=False):
                for u in units:
                    if last:
                        pe.wait_ge(slot_in[u], i * 16 + 64)
                    else:
                        pe.wait_ge(slot_in[8 + u], i * 16 + 16)
                    w = view(ring if last else dslots, u * SLOT, 2, D)
                    for cc in range(2):
                        c = 2 * u + cc
                        for g in range(groups):
                            for j in range(4):
                                b, col = bank[4 + g // 2], (g % 2) * QD
                                ins = M(b[GROUP * j:GROUP * (j + 1), col:col + QD],
                                        actT[:, g, c % 2, (c // 2) * GROUP:(c // 2 + 1) * GROUP],
                                        w[:, cc, j * QD:(j + 1) * QD],
                                        start=(c == 0 and g % 2 == 0), stop=(c == KC - 1),
                                        skip_group_check=True)
                    ins.then_inc(d_used, 1)

            def hid_turn(i, half):
                if half == 0:
                    pe.wait_ge(hid_ready, (i + 1) * GROUPS)
                for g in range(GROUPS):
                    for hh in range(2):
                        c = (g % 2) * 256 + hh * P
                        ins = TR(bank[6 + g // 2][:, c:c + P],
                                 hid[:, g, half * QD + hh * P:half * QD + (hh + 1) * P], ident)
                ins.then_inc(ht_done, 1)

            def by_groups(i, job):
                tokens = tokens_left(pe, i)
                with pe.If(tokens > 3 * GROUP):
                    job(4)
                with pe.Else():
                    with pe.If(tokens > 2 * GROUP):
                        job(3)
                    with pe.Else():
                        job(2)

            pe.wait_ge(xt_ready, 1)
            by_groups(0, lambda n: gate_up(0, n, first=True))
            pe.wait_ge(idx_ready, 3)
            xt_turn(32 * GROUPS)
            pe.wait_ge(xt_ready, 2)
            hid_turn(0, 0)
            pe.wait_ge(half_read, 1)
            hid_turn(0, 1)
            with pe.Fori(1, m + 2) as i:
                pe.wait_ge(hid_ready, i * GROUPS)
                by_groups(i, lambda n: gate_up(i, n))
                pe.wait_ge(idx_ready, i + 3)
                xt_turn(i * (16 * GROUPS) + 32 * GROUPS)
                pe.wait_ge(act_ready, i)
                pe.wait_ge(y_ready, i)

                def downs(n):
                    down(i - 1, n, (0, 1))
                    pe.wait_ge(xt_ready, i + 2)
                    hid_turn(i, 0)
                    down(i - 1, n, (2, 3))

                by_groups(i - 1, downs)
                pe.wait_ge(half_read, i * 2 + 1)
                hid_turn(i, 1)
            pe.wait_ge(act_ready, m + 2)
            pe.wait_ge(y_ready, m + 2)
            by_groups(m + 1, lambda n: down(m + 1, n, range(4), last=True))



_INS = ['x', 'attn_norm_w', 'w_in', 'gdn_conv_w', 'gdn_a_log', 'gdn_dt_bias', 'gdn_norm_w', 'cf_dw_w', 'cf_dw_b',
        'cf_ln_w', 'cf_ln_b', 'w_out', 'ffn_norm_w', 'w_router', 'b_router', 'w_gate_up', 'b_gate_up', 'w_down',
        'b_down', 'final_norm_w']


def kernel(**inputs):
    import numpy as _np
    import concourse.bacc as _bacc
    from concourse import mybir as _mybir
    from concourse.bass_utils import run_bass_kernel_spmd as _run

    nc = _bacc.Bacc("TRN2", target_bir_lowering=False, num_devices=1)
    arrays, args = {}, []
    for name in _INS:
        a = _np.ascontiguousarray(inputs[name])
        arrays[f"in_{name}_dram"] = a
        args.append(nc.dram_tensor(f"in_{name}_dram", a.shape, _mybir.dt.from_np(a.dtype), kind="ExternalInput").ap())
    shape = tuple(inputs['x'].shape)
    args.append(nc.dram_tensor("out_0_dram", shape, _mybir.dt.float32, kind="ExternalOutput").ap())
    block_kernel(nc, *args)
    r = _run(nc, [arrays], core_ids=[0])
    return r.results[0]["out_0_dram"]
```
